# Optimizing a Trainium2 kernel written in Bass

```python
import jax, jax.numpy as jnp
from jax import lax
import numpy as np

D_MODEL = 1024
BATCH = 1
SEQ = 1024
DEPTH = 2

N_MIXERS = 2
N_LAYERS_A = (DEPTH + 1) // 2
N_LAYERS_B = DEPTH // 2
CHUNK = 64
EPS = 1e-6

GDN_HEADS = 8
GDN_DK = 128
GDN_DV = 128
GDN_CONV = 4
GDN_QK = GDN_HEADS * GDN_DK
GDN_V = GDN_HEADS * GDN_DV
GDN_QKV = 2 * GDN_QK + GDN_V
GDN_IN = 2 * GDN_QK + 2 * GDN_V + 2 * GDN_HEADS

GLA_HEADS = 4
GLA_DK = D_MODEL // 2 // GLA_HEADS
GLA_DV = D_MODEL // GLA_HEADS
GLA_GATE_RANK = 16
GLA_TAU = 16.0
GLA_K = GLA_HEADS * GLA_DK
GLA_V = GLA_HEADS * GLA_DV
GLA_IN = 2 * GLA_K + 2 * GLA_V + GLA_GATE_RANK

D_FF = 2816
FFN_CONV = 3

kernel_name = "hybrid_gdn_gla_convglu_sandwich"

def rms_norm(x, g):
    xf = x.astype(jnp.float32)
    y = xf * lax.rsqrt(jnp.mean(xf * xf, axis=-1, keepdims=True) + EPS)
    return (y * g.astype(jnp.float32)).astype(x.dtype)

def l2_norm(t):
    return t * lax.rsqrt(jnp.sum(t * t, axis=-1, keepdims=True) + EPS)

def causal_depthwise_conv(x, w):
    k_width, channels = w.shape
    return lax.conv_general_dilated(
        x, w[:, None, :].astype(x.dtype), window_strides=(1,),
        padding=[(k_width - 1, 0)], dimension_numbers=('NWC', 'WIO', 'NWC'),
        feature_group_count=channels)

def heads_to_chunks(t, n_heads):
    b, s, _ = t.shape
    return t.reshape(b, s // CHUNK, CHUNK, n_heads, -1).transpose(0, 3, 1, 2, 4)

def gates_to_chunks(t):
    b, s, h = t.shape
    return t.reshape(b, s // CHUNK, CHUNK, h).transpose(0, 3, 1, 2)

def chunks_to_heads(t):
    b, h, n, c, d = t.shape
    return t.transpose(0, 2, 3, 1, 4).reshape(b, n * c, h, d)

def gated_delta_rule_chunked(q, k, v, g, beta):
    c = q.shape[-2]
    dv = v.shape[-1]
    idx = jnp.arange(c)
    causal = idx[:, None] >= idx[None, :]
    strict = idx[:, None] > idx[None, :]
    gc = jnp.cumsum(g, axis=-1)
    decay = jnp.exp(jnp.where(causal, gc[..., :, None] - gc[..., None, :], -jnp.inf))
    kb = k * beta[..., None]
    a = jnp.where(strict, jnp.einsum('bhnid,bhnjd->bhnij', kb, k) * decay, 0.0)
    eye = jnp.eye(c, dtype=q.dtype)
    rhs = jnp.concatenate([v * beta[..., None], kb * jnp.exp(gc)[..., None]], axis=-1)
    sol = lax.linalg.triangular_solve(a + eye, rhs, left_side=True, lower=True)
    u, w = sol[..., :dv], sol[..., dv:]
    qk = jnp.where(causal, jnp.einsum('bhnid,bhnjd->bhnij', q, k) * decay, 0.0)
    q_dec = q * jnp.exp(gc)[..., None]
    k_dec = k * jnp.exp(gc[..., -1:] - gc)[..., None]
    chunk_decay = jnp.exp(gc[..., -1])

    def step(state, inp):
        qk_c, qd_c, w_c, u_c, kd_c, cd_c = inp
        v_new = u_c - jnp.einsum('bhcd,bhde->bhce', w_c, state)
        o = jnp.einsum('bhcd,bhde->bhce', qd_c, state) + jnp.einsum('bhij,bhje->bhie', qk_c, v_new)
        state = state * cd_c[..., None, None] + jnp.einsum('bhcd,bhce->bhde', kd_c, v_new)
        return state, o

    xs = tuple(jnp.moveaxis(t, 2, 0) for t in (qk, q_dec, w, u, k_dec, chunk_decay))
    b, h = q.shape[0], q.shape[1]
    s0 = jnp.zeros((b, h, q.shape[-1], dv), q.dtype)
    _, o = lax.scan(step, s0, xs)
    return jnp.moveaxis(o, 0, 2)

def gla_chunked(q, k, v, log_a):
    c = q.shape[-2]
    idx = jnp.arange(c)
    causal = (idx[:, None] >= idx[None, :])[..., None]
    bc = jnp.cumsum(log_a, axis=-2)
    q_dec = q * jnp.exp(bc)
    k_dec = k * jnp.exp(bc[..., -1:, :] - bc)
    chunk_decay = jnp.exp(bc[..., -1, :])

    def step(state, inp):
        q_c, k_c, v_c, b_c, qd_c, kd_c, cd_c = inp
        rel = jnp.where(causal, b_c[:, :, :, None, :] - b_c[:, :, None, :, :], -jnp.inf)
        attn = jnp.sum(q_c[:, :, :, None, :] * k_c[:, :, None, :, :] * jnp.exp(rel), axis=-1)
        o = jnp.einsum('bhcd,bhde->bhce', qd_c, state) + jnp.einsum('bhij,bhje->bhie', attn, v_c)
        state = state * cd_c[..., :, None] + jnp.einsum('bhcd,bhce->bhde', kd_c, v_c)
        return state, o

    xs = tuple(jnp.moveaxis(t, 2, 0) for t in (q, k, v, bc, q_dec, k_dec, chunk_decay))
    b, h = q.shape[0], q.shape[1]
    s0 = jnp.zeros((b, h, q.shape[-1], v.shape[-1]), q.dtype)
    _, o = lax.scan(step, s0, xs)
    return jnp.moveaxis(o, 0, 2)

def gated_deltanet_mixer(h, w_in, conv_w, a_log, dt_bias, o_gain, w_out):
    b, s, _ = h.shape
    p = h @ w_in
    qkv = jax.nn.silu(causal_depthwise_conv(p[..., :GDN_QKV], conv_w))
    q, k, v = jnp.split(qkv.astype(jnp.float32), [GDN_QK, 2 * GDN_QK], axis=-1)
    z, b_logit, a_logit = jnp.split(p[..., GDN_QKV:], [GDN_V, GDN_V + GDN_HEADS], axis=-1)
    q = l2_norm(heads_to_chunks(q, GDN_HEADS)) * (GDN_DK ** -0.5)
    k = l2_norm(heads_to_chunks(k, GDN_HEADS))
    v = heads_to_chunks(v, GDN_HEADS)
    beta = gates_to_chunks(jax.nn.sigmoid(b_logit.astype(jnp.float32)))
    g = -jnp.exp(a_log.astype(jnp.float32)) * jax.nn.softplus(
        a_logit.astype(jnp.float32) + dt_bias.astype(jnp.float32))
    o = chunks_to_heads(gated_delta_rule_chunked(q, k, v, gates_to_chunks(g), beta))
    o = rms_norm(o, o_gain) * jax.nn.silu(z.astype(jnp.float32).reshape(b, s, GDN_HEADS, GDN_DV))
    return o.reshape(b, s, GDN_V).astype(h.dtype) @ w_out

def gla_mixer(h, w_in, w_gate_up, gate_bias, o_gain, w_out):
    b, s, _ = h.shape
    p = h @ w_in
    q, k, v, r, gate_low = jnp.split(
        p, [GLA_K, 2 * GLA_K, 2 * GLA_K + GLA_V, 2 * GLA_K + 2 * GLA_V], axis=-1)
    log_a = jax.nn.log_sigmoid((gate_low @ w_gate_up + gate_bias).astype(jnp.float32)) / GLA_TAU
    q = heads_to_chunks(q.astype(jnp.float32), GLA_HEADS) * (GLA_DK ** -0.5)
    k = heads_to_chunks(k.astype(jnp.float32), GLA_HEADS)
    v = heads_to_chunks(v.astype(jnp.float32), GLA_HEADS)
    o = chunks_to_heads(gla_chunked(q, k, v, heads_to_chunks(log_a, GLA_HEADS)))
    o = rms_norm(o, o_gain) * jax.nn.silu(r.astype(jnp.float32).reshape(b, s, GLA_HEADS, GLA_DV))
    return o.reshape(b, s, GLA_V).astype(h.dtype) @ w_out

def conv_glu_ffn(h, w_up, conv_w, w_down):
    u = causal_depthwise_conv(h @ w_up, conv_w)
    gate, val = jnp.split(u, 2, axis=-1)
    return (jax.nn.silu(gate) * val) @ w_down

def setup_inputs(seed: int = 0) -> dict:
    key = jax.random.key(seed)
    ks = jax.random.split(key, 20)
    f32 = jnp.float32
    nrm = lambda k, shape, scale: jax.random.normal(k, shape, f32) * scale
    gain = lambda k, shape: 1.0 + 0.05 * jax.random.normal(k, shape, f32)
    dt = jnp.exp(jax.random.uniform(ks[4], (N_LAYERS_A, GDN_HEADS), f32,
                                    np.log(1e-3), np.log(1e-1)))
    return {
        "x": jax.random.normal(ks[0], (BATCH, SEQ, D_MODEL), f32),
        "gdn_w_in": nrm(ks[1], (N_LAYERS_A, D_MODEL, GDN_IN), D_MODEL ** -0.5),
        "gdn_conv_w": nrm(ks[2], (N_LAYERS_A, GDN_CONV, GDN_QKV), GDN_CONV ** -0.5),
        "gdn_a_log": jnp.log(jax.random.uniform(ks[3], (N_LAYERS_A, GDN_HEADS), f32, 1.0, 16.0)),
        "gdn_dt_bias": dt + jnp.log(-jnp.expm1(-dt)),
        "gdn_o_norm": gain(ks[5], (N_LAYERS_A, GDN_DV)),
        "gdn_w_out": nrm(ks[6], (N_LAYERS_A, GDN_V, D_MODEL), GDN_V ** -0.5),
        "gla_w_in": nrm(ks[7], (N_LAYERS_B, D_MODEL, GLA_IN), D_MODEL ** -0.5),
        "gla_w_gate_up": nrm(ks[8], (N_LAYERS_B, GLA_GATE_RANK, GLA_K), GLA_GATE_RANK ** -0.5),
        "gla_gate_bias": nrm(ks[9], (N_LAYERS_B, GLA_K), 0.1),
        "gla_o_norm": gain(ks[10], (N_LAYERS_B, GLA_DV)),
        "gla_w_out": nrm(ks[11], (N_LAYERS_B, GLA_V, D_MODEL), GLA_V ** -0.5),
        "mix_pre_norm": gain(ks[12], (DEPTH, D_MODEL)),
        "mix_post_norm": gain(ks[13], (DEPTH, D_MODEL)),
        "ffn_pre_norm": gain(ks[14], (DEPTH, D_MODEL)),
        "ffn_post_norm": gain(ks[15], (DEPTH, D_MODEL)),
        "ffn_w_up": nrm(ks[16], (DEPTH, D_MODEL, 2 * D_FF), D_MODEL ** -0.5),
        "ffn_conv_w": nrm(ks[17], (DEPTH, FFN_CONV, 2 * D_FF), FFN_CONV ** -0.5),
        "ffn_w_down": nrm(ks[18], (DEPTH, D_FF, D_MODEL), D_FF ** -0.5),
    }

def reference(x, gdn_w_in, gdn_conv_w, gdn_a_log, gdn_dt_bias, gdn_o_norm, gdn_w_out,
              gla_w_in, gla_w_gate_up, gla_gate_bias, gla_o_norm, gla_w_out,
              mix_pre_norm, mix_post_norm, ffn_pre_norm, ffn_post_norm,
              ffn_w_up, ffn_conv_w, ffn_w_down):
    for layer in range(DEPTH):
        j = layer // N_MIXERS
        hn = rms_norm(x, mix_pre_norm[layer])
        if layer % N_MIXERS == 0:
            m = gated_deltanet_mixer(hn, gdn_w_in[j], gdn_conv_w[j], gdn_a_log[j],
                                     gdn_dt_bias[j], gdn_o_norm[j], gdn_w_out[j])
        else:
            m = gla_mixer(hn, gla_w_in[j], gla_w_gate_up[j], gla_gate_bias[j],
                          gla_o_norm[j], gla_w_out[j])
        x = x + rms_norm(m, mix_post_norm[layer])
        f = conv_glu_ffn(rms_norm(x, ffn_pre_norm[layer]), ffn_w_up[layer],
                         ffn_conv_w[layer], ffn_w_down[layer])
        x = x + rms_norm(f, ffn_post_norm[layer])
    return x


_drawn_inputs = setup_inputs


def setup_inputs(seed=0):
    import zlib

    import numpy as np

    out = dict(_drawn_inputs(seed))
    spreads = {}
    factors = {}
    for name, (base, spread) in spreads.items():
        noise = np.random.default_rng([zlib.crc32(name.encode()), seed]).standard_normal(out[name].shape)
        drawn = base * np.exp(spread * noise) if base else spread * noise
        out[name] = __import__('jax').numpy.asarray(drawn.astype(out[name].dtype))
    for name, factor in factors.items():
        out[name] = (out[name] * factor).astype(out[name].dtype)
    return out
```

```python
from contextlib import ExitStack

import concourse.bass as bass
from concourse import mybir

P = 128
T = 1024
D = 1024
KT = D // P
NT = T // P
HALF = 512
EPS = 1e-6

F32 = mybir.dt.float32
F32R = mybir.dt.float32r
ACT = mybir.ActivationFunctionType
ALU = mybir.AluOpType
AX_X = mybir.AxisListType.X

D_FF = 2816
FT = D_FF // P
UP_TILES = 2 * FT
PAIR = 2
GROUPS = FT // PAIR
FFN_TAPS = 3
RING = 3


def buffers(nc, ctx):
    def sb(name, shape, dt=F32):
        return ctx.enter_context(nc.sbuf_tensor(name, shape, dt))

    def ps(name, shape, dt=F32):
        return ctx.enter_context(nc.psum_tensor(name, shape, dt))

    return sb, ps


def semaphores(nc, ctx, tag):
    made = []

    def sem(name):
        made.append(ctx.enter_context(nc.semaphore(tag + name)))
        return made[-1]

    def clear():
        for s in made:
            nc.gpsimd.sem_clear(s)
        nc.all_engine_barrier()

    ctx.callback(clear)
    return sem


def product3(pe, out, w_hi, w_lo, x_hi, x_lo, first, last):
    pe.matmul(out, w_hi, x_hi, start=first, stop=False)
    pe.matmul(out, w_hi, x_lo, start=False, stop=False)
    return pe.matmul(out, w_lo, x_hi, start=False, stop=last)


def ffn(nc, layer, w_up, conv_w, w_down, x_hi, x_lo, acc):
    ctx = ExitStack()
    with ctx:
        sb, ps = buffers(nc, ctx)
        n_ = f"f{layer}_"
        sem = semaphores(nc, ctx, n_)
        raw = [sb(f"{n_}raw{i}", [P, D]) for i in range(RING)]
        w_hi = [sb(f"{n_}whi{i}", [P, D], F32R) for i in range(RING)]
        w_lo = [sb(f"{n_}wlo{i}", [P, D], F32R) for i in range(RING)]
        pad = FFN_TAPS - 1
        u = [sb(f"{n_}u{i}", [P, pad + T]) for i in range(2)]
        gate = sb(f"{n_}gate", [P, T])
        hid = sb(f"{n_}hid", [P, T])
        h_hi = [sb(f"{n_}hhi{i}", [P, T], F32R) for i in range(PAIR)]
        h_lo = [sb(f"{n_}hlo{i}", [P, T], F32R) for i in range(PAIR)]
        taps = sb(f"{n_}taps", [P, UP_TILES, FFN_TAPS])
        up_ps = [ps(f"{n_}up{i}", [P, T]) for i in range(2)]
        down_ps = [ps(f"{n_}down{i}", [P, HALF]) for i in range(4)]

        s_raw = [sem(f"w_raw{i}") for i in range(RING)]
        s_hi = sem("w_high")
        s_lo = sem("w_low")
        s_up = sem("up_product_done")
        s_taps = sem("taps_loaded")
        s_zero = sem("ffn_zeroed")
        s_u = sem("u_evicted")
        s_conv = sem("conv_done")
        s_silu = sem("gate_activated")
        s_h = sem("hidden_made")
        s_hhi = sem("hidden_high")
        s_hlo = sem("hidden_low")
        s_bank = sem("down_bank_full")
        s_free = sem("down_bank_free")

        def slot(c):
            return c % RING

        def turn(g, c):
            return 2 * g + c // RING

        def first_pair(g):
            return (0, 1) if isinstance(g, int) and g == 0 else (-2, -1)

        block = ctx.enter_context(nc.Block())

        def groups(engine, body, after):
            body(0)
            with engine.Fori(1, GROUPS) as g:
                body(g)
            after(GROUPS)

        @block.sync
        def _(sp):
            def load(g, c, source):
                if not (isinstance(g, int) and 6 * g + c < RING):
                    sp.wait_ge(s_lo, 6 * g + c - RING + 1)
                sp.dma_start(raw[slot(c)][:, :], source.rearrange("a p f -> p (a f)")) \
                    .then_inc(s_raw[slot(c)], 16)

            def up(g, c, j, value):
                load(g, c, w_up[layer, bass.ds(g * PAIR + j + value * FT, 1), :, :])

            def down(g, c, j):
                load(g, c, w_down[layer, bass.ds(g * PAIR + j - PAIR, 1), :, :])

            def body(g):
                c = first_pair(g)
                up(g, c[0], 0, 0)
                up(g, c[1], 0, 1)
                if not isinstance(g, int):
                    down(g, 0, 0)
                    down(g, 1, 1)
                up(g, 2, 1, 0)
                up(g, 3, 1, 1)

            sp.dma_start(taps[:, :, :], conv_w[layer]).then_inc(s_taps, 16)
            groups(sp, body, lambda g: (down(g, -2, 0), down(g, -1, 1)))

        @block.gpsimd
        def _(pool):
            pool.memset(acc[:, :, :], 0.0)
            pool.memset(u[0][:, 0:pad], 0.0)
            pool.memset(u[1][:, 0:pad], 0.0)
            pool.drain().then_inc(s_zero, 1)

            def split(g, c):
                pool.wait_ge(s_hi, 6 * g + c + 1)
                k = slot(c)
                pool.tensor_tensor(w_lo[k][:, :], raw[k][:, :], w_hi[k][:, :].bitcast(F32), ALU.subtract) \
                    .then_inc(s_lo, 1)

            def body(g):
                for c in ((0, 1, 2, 3) if isinstance(g, int) else (-2, -1, 0, 1, 2, 3)):
                    split(g, c)

            groups(pool, body, lambda g: (split(g, -2), split(g, -1)))

        @block.scalar
        def _(act):
            def high(g, c):
                act.wait_ge(s_raw[slot(c)], 16 * turn(g, c) + 16)
                if isinstance(g, int):
                    if c >= RING:
                        act.wait_ge(s_up, c - RING + 1)
                elif c in (3, 4):
                    act.wait_ge(s_bank, 2 * NT * g)
                else:
                    act.wait_ge(s_up, 4 * g + (0, 1, 2, None, None, 3)[c])
                act.activation(w_hi[slot(c)][:, :], raw[slot(c)][:, :], ACT.Copy).then_inc(s_hi, 1)

            def evict(g, k):
                act.wait_ge(s_up, 4 * g + k + 1)
                if not (isinstance(g, int) and 4 * g + k < 2):
                    act.wait_ge(s_conv, 4 * g + k - 1)
                act.activation(u[k % 2][:, pad:], up_ps[k % 2][:, :], ACT.Copy).then_inc(s_u, 1)

            def silu(g, j):
                act.wait_ge(s_conv, 4 * g + 2 * j + 1)
                act.activation(gate[:, :], gate[:, :], ACT.Silu).then_inc(s_silu, 1)

            def hidden_high(g, j):
                act.wait_ge(s_h, 2 * g + j + 1)
                if j == 0 and not isinstance(g, int):
                    act.wait_ge(s_bank, 2 * NT * g)
                act.activation(h_hi[j][:, :], hid[:, :], ACT.Copy).then_inc(s_hhi, 1)

            high(0, 0)
            high(0, 1)

            def body(g):
                first = isinstance(g, int)
                if not first:
                    evict(g - 1, 3)
                    high(g, 0)
                    hidden_high(g - 1, 1)
                evict(g, 0)
                high(g, 3 if first else 1)
                silu(g, 0)
                evict(g, 1)
                if first:
                    high(g, 4)
                    hidden_high(g, 0)
                else:
                    high(g, 2)
                    high(g, 3)
                    hidden_high(g, 0)
                    high(g, 4)
                evict(g, 2)
                high(g, 5)
                silu(g, 1)

            high(0, 2)
            groups(act, body, lambda g: (evict(g - 1, 3), hidden_high(g - 1, 1)))

        @block.vector
        def _(dve):
            def conv(g, k, out):
                dve.wait_ge(s_u, 4 * g + k + 1)
                w = taps[:, bass.ds(g * PAIR + k // 2 + (k % 2) * FT, 1), :]
                src = u[k % 2]
                dve.tensor_scalar(out[:, :], src[:, 2:2 + T], w[:, 0, 2:3], None, ALU.mult)
                dve.drain()
                dve.scalar_tensor_tensor(out=out[:, :], in0=src[:, 1:1 + T], scalar=w[:, 0, 1:2],
                                         in1=out[:, :], op0=ALU.mult, op1=ALU.add)
                dve.drain()
                dve.scalar_tensor_tensor(out=out[:, :], in0=src[:, 0:T], scalar=w[:, 0, 0:1],
                                         in1=out[:, :], op0=ALU.mult, op1=ALU.add).then_inc(s_conv, 1)

            def hidden(g, j):
                conv(g, 2 * j + 1, hid)
                dve.drain()
                dve.wait_ge(s_silu, 2 * g + j + 1)
                dve.tensor_tensor(hid[:, :], hid[:, :], gate[:, :], ALU.mult).then_inc(s_h, 1)

            def hidden_low(g, j):
                dve.drain()
                dve.wait_ge(s_hhi, 2 * g + j + 1)
                dve.tensor_tensor(h_lo[j][:, :], hid[:, :], h_hi[j][:, :].bitcast(F32), ALU.subtract) \
                    .then_inc(s_hlo, 1)
                dve.drain()

            def add_down(g):
                for b in range(2 * NT):
                    dve.wait_ge(s_bank, 2 * NT * g + b + 1)
                    part = acc[:, b // 2, (b % 2) * HALF:(b % 2 + 1) * HALF]
                    dve.tensor_tensor(part, down_ps[b % 4][:, :], part, ALU.add).then_inc(s_free, 1)

            dve.wait_ge(s_taps, 16)
            dve.wait_ge(s_zero, 1)
            dve.drain().then_inc(s_free, 4)

            def body(g):
                if not isinstance(g, int):
                    hidden(g - 1, 1)
                    hidden_low(g - 1, 1)
                conv(g, 0, gate)
                hidden(g, 0)
                if not isinstance(g, int):
                    add_down(g - 1)
                hidden_low(g, 0)
                conv(g, 2, gate)

            groups(dve, body, lambda g: (hidden(g - 1, 1), hidden_low(g - 1, 1), add_down(g - 1)))

        @block.tensor
        def _(pe):
            def up(g, c, k):
                pe.wait_ge(s_lo, 6 * g + c + 1)
                if not (isinstance(g, int) and 4 * g + k < 2):
                    pe.wait_ge(s_u, 4 * g + k - 1)
                s = slot(c)
                for half in range(2):
                    cols = slice(half * HALF, (half + 1) * HALF)
                    for kt in range(KT):
                        f = slice(kt * P, (kt + 1) * P)
                        last = product3(pe, up_ps[k % 2][:, cols], w_hi[s][:, f], w_lo[s][:, f],
                                        x_hi[:, kt, cols], x_lo[:, kt, cols], kt == 0, kt == KT - 1)
                last.then_inc(s_up, 1)

            def down(g, c):
                pe.wait_ge(s_lo, 6 * g + 6 + c + 2)
                pe.wait_ge(s_hlo, 2 * g + 2)
                for b in range(2 * NT):
                    pe.wait_ge(s_free, 2 * NT * g + b + 1)
                    rows = slice(b // 2 * P, (b // 2 + 1) * P)
                    cols = slice((b % 2) * HALF, (b % 2 + 1) * HALF)
                    for j in range(PAIR):
                        s = slot(c + j)
                        last = product3(pe, down_ps[b % 4][:, :], h_hi[j][:, rows], h_lo[j][:, rows],
                                        w_hi[s][:, cols], w_lo[s][:, cols], j == 0, j == PAIR - 1)
                    last.then_inc(s_bank, 1)

            def body(g):
                c = first_pair(g)
                up(g, c[0], 0)
                up(g, c[1], 1)
                if not isinstance(g, int):
                    down(g - 1, 0)
                up(g, 2, 2)
                up(g, 3, 3)

            groups(pe, body, lambda g: down(g - 1, -2))


def token_pass(nc, tag, consts, x_in, x_out, post_gain, pre_gain, x_hi, x_lo, acc=None, mixed=None, w_out=None):
    ident, eps = consts["ident"], consts["eps"]
    ctx = ExitStack()
    with ctx:
        sb, ps = buffers(nc, ctx)
        n_ = tag + "_"
        sem = semaphores(nc, ctx, n_)

        def two(name, shape, dt=F32):
            return [sb(f"{n_}{name}{i}", shape, dt) for i in range(2)]

        xt, xn, xs, xg = (two(x, [P, D]) for x in ("xt", "xn", "xs", "xg"))
        junk = sb(n_ + "squares", [P, D])
        ss, std, rms = (two(x, [P, 2]) for x in ("ss", "std", "rms"))
        post = sb(n_ + "post", [P, D])
        pre = sb(n_ + "pre", [P, KT])
        turned = [ps(f"{n_}turned{i}", [P, KT, P]) for i in range(2)]
        s_gain = sem("gains_loaded")
        s_xin = [sem(f"x_arrived{i}") for i in range(2)]
        s_xout = [sem(f"x_stored{i}") for i in range(2)]
        s_mstd = sem("m_deviation")
        s_xn = sem("x_updated")
        s_xstd = sem("x_deviation")
        s_xs = sem("x_normed")
        s_turn = sem("x_turned")
        s_xg = sem("x_gained")
        s_xhi = sem("x_high")
        s_xlo = sem("x_low")
        if w_out is not None:
            w_raw = two("wraw", [P, D])
            w_hi = sb(n_ + "whi", [P, KT, D], F32R)
            w_lo = sb(n_ + "wlo", [P, KT, D], F32R)
            o_raw = two("oraw", [P, KT, P])
            o_hi = two("ohi", [P, KT, P], F32R)
            o_lo = two("olo", [P, KT, P], F32R)
            m_ps = [ps(f"{n_}m{i}", [P, D]) for i in range(2)]
            s_wraw = [sem(f"w_raw{i}") for i in range(2)]
            s_whi, s_wlo = sem("w_high"), sem("w_low")
            s_oraw = [sem(f"mixed_arrived{i}") for i in range(2)]
            s_ohi, s_olo = sem("mixed_high"), sem("mixed_low")
            s_m = sem("m_product_done")

        def m_of(c, s):
            if w_out is not None:
                return m_ps[s][:, :]
            return acc[:, bass.ds(c, 1), :].rearrange("p a d -> p (a d)")

        updated = xn if post_gain is not None else xt
        block = ctx.enter_context(nc.Block())

        @block.sync
        def _(sp):
            def load(c, s):
                sp.dma_start(xt[s][:, :], x_in[bass.ds(c, 1), :, :].rearrange("a p d -> p (a d)")) \
                    .then_inc(s_xin[s], 16)
                if w_out is not None:
                    if not isinstance(c, int):
                        sp.wait_ge(s_olo, c - 1)
                    sp.dma_start(o_raw[s][:, :, :], mixed[:, :, bass.ds(c * P, P)].rearrange("k p t -> p k t")) \
                        .then_inc(s_oraw[s], 16)

            def store(c, s):
                if x_out is not None:
                    sp.wait_ge(s_xn, c + 1)
                    sp.dma_start(x_out[bass.ds(c, 1), :, :].rearrange("a p d -> p (a d)"), xn[s][:, :]) \
                        .then_inc(s_xout[s], 16)
                else:
                    sp.wait_ge(s_xs, c + 1)

            sp.dma_start(pre[:, :], (pre_gain if pre_gain is not None else consts["any_gain"])) \
                .then_inc(s_gain, 16)
            if post_gain is not None:
                sp.dma_start(post[:, :], post_gain.partition_broadcast(P)).then_inc(s_gain, 16)
            load(0, 0)
            load(1, 1)
            if w_out is not None:
                for kt in range(KT):
                    if kt >= 2:
                        sp.wait_ge(s_wlo, kt - 1)
                    sp.dma_start(w_raw[kt % 2][:, :], w_out[kt]).then_inc(s_wraw[kt % 2], 16)
            with sp.Fori(0, NT // 2 - 1) as i:
                for s in range(2):
                    store(i * 2 + s, s)
                    load(i * 2 + s + 2, s)
            for s in range(2):
                store(NT - 2 + s, s)
            if x_out is not None:
                for s in range(2):
                    sp.wait_ge(s_xout[s], 16 * (NT // 2))

        def pairs(body):
            def run(engine):
                body(0, [0, 1])
                with engine.Fori(1, NT // 2) as i:
                    body(i, [i * 2, i * 2 + 1])
            return run

        @block.scalar
        def _(act):
            if w_out is not None:
                for kt in range(KT):
                    act.wait_ge(s_wraw[kt % 2], 16 * (kt // 2 + 1))
                    act.activation(w_hi[:, kt, :], w_raw[kt % 2][:, :], ACT.Copy).then_inc(s_whi, 1)

            def body(i, c):
                first = isinstance(i, int)
                if w_out is not None:
                    for s in range(2):
                        act.wait_ge(s_oraw[s], 16 * i + 16)
                        if not first:
                            act.wait_ge(s_m, c[s] - 1)
                        act.activation(o_hi[s][:, :, :], o_raw[s][:, :, :], ACT.Copy).then_inc(s_ohi, 1)
                if post_gain is not None:
                    for s in range(2):
                        if w_out is not None:
                            act.wait_ge(s_m, c[s] + 1)
                        if not first:
                            act.wait_ge(s_xn, c[s] - 1)
                        act.activation(junk[:, :], m_of(c[s], s), ACT.Square, accum_out=ss[s][:, 0:1])
                        act.drain()
                        act.activation(std[s][:, 0:1], ss[s][:, 0:1], ACT.Sqrt, scale=1.0 / D,
                                       bias=eps[:, 0:1]).then_inc(s_mstd, 1)
                if pre_gain is None:
                    return
                for s in range(2):
                    if post_gain is not None:
                        act.wait_ge(s_xn, c[s] + 1)
                    else:
                        act.wait_ge(s_xin[s], 16 * i + 16)
                    act.activation(junk[:, :], updated[s][:, :], ACT.Square, accum_out=ss[s][:, 1:2])
                    act.drain()
                    act.activation(std[s][:, 1:2], ss[s][:, 1:2], ACT.Sqrt, scale=1.0 / D,
                                   bias=eps[:, 0:1]).then_inc(s_xstd, 1)
                for s in range(2):
                    act.wait_ge(s_xg, c[s] + 1)
                    act.activation(x_hi[:, :, bass.ds(c[s] * P, P)],
                                   xg[s][:, :].rearrange("p (k t) -> p k t", k=KT), ACT.Copy) \
                        .then_inc(s_xhi, 1)

            pairs(body)(act)

        @block.gpsimd
        def _(pool):
            if w_out is not None:
                for kt in range(KT):
                    pool.wait_ge(s_whi, kt + 1)
                    pool.tensor_tensor(w_lo[:, kt, :], w_raw[kt % 2][:, :], w_hi[:, kt, :].bitcast(F32),
                                       ALU.subtract).then_inc(s_wlo, 1)

            def body(i, c):
                if w_out is not None:
                    for s in range(2):
                        pool.wait_ge(s_ohi, c[s] + 1)
                        pool.tensor_tensor(o_lo[s][:, :, :], o_raw[s][:, :, :], o_hi[s][:, :, :].bitcast(F32),
                                           ALU.subtract).then_inc(s_olo, 1)
                if pre_gain is None:
                    return
                for s in range(2):
                    pool.wait_ge(s_xhi, c[s] + 1)
                    at = bass.ds(c[s] * P, P)
                    pool.tensor_tensor(x_lo[:, :, at], xg[s][:, :].rearrange("p (k t) -> p k t", k=KT),
                                       x_hi[:, :, at].bitcast(F32), ALU.subtract).then_inc(s_xlo, 1)

            pairs(body)(pool)

        @block.vector
        def _(dve):
            dve.wait_ge(s_gain, 32 if post_gain is not None else 16)

            def body(i, c):
                first = isinstance(i, int)
                if post_gain is not None:
                    for s in range(2):
                        dve.wait_ge(s_mstd, c[s] + 1)
                        dve.reciprocal(rms[s][:, 0:1], std[s][:, 0:1])
                        dve.drain()
                        if not first:
                            dve.wait_ge(s_xout[s], 16 * i)
                        dve.scalar_tensor_tensor(out=xn[s][:, :], in0=m_of(c[s], s), scalar=rms[s][:, 0:1],
                                                 in1=post[:, :], op0=ALU.mult, op1=ALU.mult)
                        dve.drain()
                        dve.wait_ge(s_xin[s], 16 * i + 16)
                        dve.tensor_tensor(xn[s][:, :], xn[s][:, :], xt[s][:, :], ALU.add).then_inc(s_xn, 1)
                if pre_gain is None:
                    return
                for s in range(2):
                    dve.wait_ge(s_xstd, c[s] + 1)
                    dve.reciprocal(rms[s][:, 1:2], std[s][:, 1:2])
                    dve.drain()
                    dve.tensor_scalar(xs[s][:, :], updated[s][:, :], rms[s][:, 1:2], None, ALU.mult) \
                        .then_inc(s_xs, 1)
                for s in range(2):
                    dve.wait_ge(s_turn, c[s] + 1)
                    if not first:
                        dve.wait_ge(s_xlo, c[s] - 1)
                    dve.tensor_tensor(xg[s][:, :].rearrange("p (k t) -> p k t", k=KT), turned[s][:, :, :],
                                      pre[:, :].unsqueeze(2).to_broadcast([P, KT, P]), ALU.mult) \
                        .then_inc(s_xg, 1)

            pairs(body)(dve)

        @block.tensor
        def _(pe):
            if w_out is not None:
                pe.wait_ge(s_wlo, KT)

            def body(i, c):
                first = isinstance(i, int)
                if w_out is not None:
                    for s in range(2):
                        pe.wait_ge(s_olo, c[s] + 1)
                        if not first:
                            pe.wait_ge(s_xn, c[s] - 1)
                        for half in range(2):
                            cols = slice(half * HALF, (half + 1) * HALF)
                            for kt in range(KT):
                                last = product3(pe, m_ps[s][:, cols], o_hi[s][:, kt, :], o_lo[s][:, kt, :],
                                                w_hi[:, kt, cols], w_lo[:, kt, cols], kt == 0, kt == KT - 1)
                        last.then_inc(s_m, 1)
                if pre_gain is None:
                    return
                for s in range(2):
                    pe.wait_ge(s_xs, c[s] + 1)
                    for kt in range(KT):
                        last = pe.transpose(turned[s][:, kt, :], xs[s][:, kt * P:(kt + 1) * P], ident[:, :])
                    last.then_inc(s_turn, 1)

            pairs(body)(pe)


def constants(nc, ctx):
    sb, _ = buffers(nc, ctx)
    ident = sb("ident", [P, P])
    upper = sb("upper", [P, P])
    ones = sb("ones", [P, P])
    eps = sb("eps", [P, 1])
    sizes = tuple(2 ** n for n in range(7))
    masks = sb("masks", [P, len(sizes), P])
    with nc.Block() as block:
        @block.gpsimd
        def _(pool):
            for n, s in enumerate(sizes):
                pool.memset(masks[:, n, :], 1.0)
            pool.drain()
            for n, s in enumerate(sizes):
                blocks = P // (2 * s)
                m = masks[:, n, :].rearrange("p (b half t) -> p b half t", half=2, t=s)
                pool.memset(m[:, :, 0, :], 0.0)
                for pattern, base, mult in (([[-2 * s, blocks], [0, s]], 0, 1),
                                            ([[2 * s, blocks], [0, s]], s - 1, -1)):
                    pool.drain()
                    pool.affine_select(out=m[:, :, 1, :], in_=m[:, :, 1, :], compare_op=ALU.is_ge, fill=0.0,
                                       base=base, pattern=pattern, channel_multiplier=mult)
            pool.memset(ident[:, :], 0.0)
            pool.memset(upper[:, :], 1.0)
            pool.memset(ones[:, :], 1.0)
            pool.memset(eps[:, :], EPS)
            pool.drain()
            pool.affine_select(out=ident[:, :], in_=ident[:, :], compare_op=ALU.not_equal, fill=1.0, base=0,
                               pattern=[[-1, P]], channel_multiplier=1)
            pool.affine_select(out=upper[:, :], in_=upper[:, :], compare_op=ALU.is_ge, fill=0.0, base=0,
                               pattern=[[1, P]], channel_multiplier=-1)
    return dict(ident=ident, upper=upper, ones=ones, eps=eps, masks=masks)


GDN_HEADS = 8
GDN_TAPS = 4
GATE_KINDS = 6
G_LOG, G_BETA, G_CUM, G_CUM_EXP, G_TO_END, G_CHUNK = range(GATE_KINDS)
LEVELS = (2, 4, 8, 16, 32, 64)
SLOTS = 2


def token_logits(pe, out, x_hi, x_lo, w_hi, w_lo):
    for c in range(NT):
        t = slice(c * P, (c + 1) * P)
        for kt in range(KT):
            last = product3(pe, out[:, c, :], x_hi[:, kt, t], x_lo[:, kt, t], w_hi[:, kt, :],
                            w_lo[:, kt, :], kt == 0, kt == KT - 1)
    return last


def gdn_gates(nc, consts, w_small, a_log, dt_bias, x_hi, x_lo, gates):
    ctx = ExitStack()
    with ctx:
        sb, ps = buffers(nc, ctx)
        sem = semaphores(nc, ctx, "ga_")
        raw = sb("ga_raw", [P, KT, 2 * GDN_HEADS])
        w_hi = sb("ga_whi", [P, KT, 2 * GDN_HEADS], F32R)
        w_lo = sb("ga_wlo", [P, KT, 2 * GDN_HEADS], F32R)
        alog = sb("ga_alog", [P, GDN_HEADS])
        dt = sb("ga_dt", [P, GDN_HEADS])
        y, a, e, f, g = (sb(f"ga_{x}", [P, GDN_HEADS, NT]) for x in ("y", "a", "e", "f", "g"))
        logits = ps("ga_logits", [P, NT, 2 * GDN_HEADS])
        cum = ps("ga_cum", [P, GDN_HEADS, NT])
        total = ps("ga_total", [P, GDN_HEADS, NT])
        s_raw, s_hi, s_lo = sem("w_raw"), sem("w_high"), sem("w_low")
        s_done = sem("gate_logits_done")
        s_in = sem("rates_loaded")
        s_y = sem("gate_input_made")
        s_exp = sem("gate_exps_made")
        s_g = sem("log_decay_made")
        s_cum = sem("decay_summed")
        s_rest = sem("decay_relative")
        b_view = logits[:, :, 0:GDN_HEADS].rearrange("p c h -> p h c")
        a_view = logits[:, :, GDN_HEADS:2 * GDN_HEADS].rearrange("p c h -> p h c")
        block = ctx.enter_context(nc.Block())

        @block.sync
        def _(sp):
            sp.dma_start(raw[:, :, :], w_small).then_inc(s_raw, 16)
            sp.dma_start(alog[:, :], a_log.partition_broadcast(P)).then_inc(s_in, 16)
            sp.dma_start(dt[:, :], dt_bias.partition_broadcast(P)).then_inc(s_in, 16)

        @block.scalar
        def _(act):
            act.wait_ge(s_raw, 16)
            act.activation(w_hi[:, :, :], raw[:, :, :], ACT.Copy).then_inc(s_hi, 1)
            act.wait_ge(s_in, 32)
            act.activation(alog[:, :], alog[:, :], ACT.Exp)
            act.wait_ge(s_y, 1)
            act.activation(f[:, :, :], f[:, :, :], ACT.Exp)
            act.activation(e[:, :, :], a[:, :, :], ACT.Exp, scale=-1.0)
            act.drain()
            act.activation(e[:, :, :], e[:, :, :], ACT.Ln, bias=consts["ones"][:, 0:1]).then_inc(s_exp, 1)
            act.wait_ge(s_rest, 1)
            act.activation(gates[:, :, G_CUM_EXP, :], gates[:, :, G_CUM, :], ACT.Exp)
            act.activation(gates[:, :, G_TO_END, :], a[:, :, :], ACT.Exp)
            act.activation(gates[:, :, G_CHUNK, :], total[:, :, :], ACT.Exp)

        @block.vector
        def _(dve):
            dve.wait_ge(s_hi, 1)
            dve.tensor_tensor(w_lo[:, :, :], raw[:, :, :], w_hi[:, :, :].bitcast(F32), ALU.subtract) \
                .then_inc(s_lo, 1)
            dve.wait_ge(s_in, 32)
            dve.wait_ge(s_done, 1)
            dve.tensor_scalar(f[:, :, :], b_view, -1.0, None, ALU.mult)
            dve.tensor_tensor(y[:, :, :], a_view, dt[:, :].unsqueeze(2).to_broadcast([P, GDN_HEADS, NT]), ALU.add)
            dve.drain()
            dve.scalar_tensor_tensor(out=a[:, :, :], in0=y[:, :, :], scalar=-1.0, in1=y[:, :, :],
                                     op0=ALU.mult, op1=ALU.max).then_inc(s_y, 1)
            dve.wait_ge(s_exp, 1)
            dve.scalar_tensor_tensor(out=y[:, :, :], in0=y[:, :, :], scalar=0.0, in1=e[:, :, :],
                                     op0=ALU.max, op1=ALU.add)
            dve.tensor_scalar(f[:, :, :], f[:, :, :], 1.0, None, ALU.add)
            dve.drain()
            dve.scalar_tensor_tensor(out=g[:, :, :], in0=y[:, :, :], scalar=-1.0,
                                     in1=alog[:, :].unsqueeze(2).to_broadcast([P, GDN_HEADS, NT]),
                                     op0=ALU.mult, op1=ALU.mult).then_inc(s_g, 1)
            dve.drain()
            dve.tensor_copy(gates[:, :, G_LOG, :], g[:, :, :])
            dve.reciprocal(gates[:, :, G_BETA, :], f[:, :, :])
            dve.wait_ge(s_cum, 1)
            dve.tensor_copy(gates[:, :, G_CUM, :], cum[:, :, :])
            dve.drain()
            dve.tensor_tensor(a[:, :, :], total[:, :, :], gates[:, :, G_CUM, :], ALU.subtract) \
                .then_inc(s_rest, 1)

        @block.tensor
        def _(pe):
            pe.wait_ge(s_lo, 1)
            token_logits(pe, logits, x_hi, x_lo, w_hi, w_lo).then_inc(s_done, 1)
            pe.wait_ge(s_g, 1)
            flat = g[:, :, :].rearrange("p h c -> p (h c)")
            pe.matmul(cum[:, :, :].rearrange("p h c -> p (h c)"), consts["upper"][:, :], flat, start=True, stop=True)
            pe.matmul(total[:, :, :].rearrange("p h c -> p (h c)"), consts["ones"][:, :], flat,
                      start=True, stop=True).then_inc(s_cum, 1)


def wide(column, n=P):
    return column.unsqueeze(2).to_broadcast([P, column.shape[1], n])


def each(mask, n=NT):
    return mask.unsqueeze(1).to_broadcast([P, n, mask.shape[1]])


def gdn(nc, consts, w_in, conv_w, o_gain, gates, x_hi, x_lo, mixed):
    ident, upper, eps = consts["ident"], consts["upper"], consts["eps"]
    ctx = ExitStack()
    with ctx:
        sb, ps = buffers(nc, ctx)
        sem = semaphores(nc, ctx, "g_")
        H = GDN_HEADS
        raw = [sb(f"g_raw{i}", [P, D]) for i in range(SLOTS)]
        w_hi = [sb(f"g_whi{i}", [P, D], F32R) for i in range(SLOTS)]
        w_lo = [sb(f"g_wlo{i}", [P, D], F32R) for i in range(SLOTS)]
        pad = GDN_TAPS - 1
        u = [sb(f"g_u{i}", [P, pad + T]) for i in range(2)]
        taps = sb("g_taps", [P, 3 * H, GDN_TAPS])
        qkv = [sb(f"g_{x}T", [P, T]) for x in "qkv"]
        z = sb("g_z", [P, T])

        def chunks(name):
            return sb("g_" + name, [P, NT, P])

        kn = chunks("kn")
        kb = chunks("kb")
        qn = chunks("qn")
        vb = chunks("vb")
        knT = chunks("knT")
        kqT = sb("g_kqT", [P, NT, 2 * P])
        decay = chunks("decay")
        attn = chunks("attn")
        aT = chunks("aT")
        inv = chunks("inv")
        invT = chunks("invT")
        cT = [chunks(f"cT{i}") for i in range(2)]
        from_start = cT[1]
        m1 = chunks("m1")
        wTn = chunks("wTn")
        qdT = chunks("qdT")
        zc = sb("g_zc", [P, T])
        on = chunks("on")
        og = sb("g_og", [P, T])
        vn = [sb(f"g_vn{i}", [P, P]) for i in range(2)]
        state = sb("g_state", [P, P])
        hg = sb("g_hg", [P, GATE_KINDS, NT])
        chunk_decay = sb("g_cd", [P, NT])
        gain = sb("g_gain", [P, 1])
        ss, std, rs = (sb(f"g_{x}", [P, 2 * NT]) for x in ("ss", "std", "rs"))
        sso, stdo, rso = (sb(f"g_{x}", [P, NT]) for x in ("sso", "stdo", "rso"))
        masks = consts["masks"]

        pa = ps("g_pa", [P, T])
        pm = ps("g_pm", [P, T])
        pt = ps("g_pt", [P, 2 * T])

        def by_chunk(psum, at=0):
            return psum[:, at:at + T].rearrange("p (c t) -> p c t", c=NT)

        s_raw = [sem(f"w_raw{i}") for i in range(SLOTS)]
        s_hi, s_lo = sem("w_high"), sem("w_low")
        s_taps = sem("taps_loaded")
        s_set = sem("pads_set")
        s_a = sem("projection_half_done")
        s_u = sem("projection_half_evicted")
        s_conv, s_silu = sem("conv_done"), sem("conv_activated")
        s_tok = sem("token_major_in_psum")
        s_sq, s_ss, s_std = sem("squares_made"), sem("squares_summed"), sem("deviation_made")
        s_nrm = sem("normed")
        s_ft = sem("feature_major_in_psum")
        s_kq = sem("feature_major_made")
        s_gb, s_gcb = sem("log_decay_repeated"), sem("decay_by_columns_in_psum")
        s_dm, s_dx = sem("decay_exponent_made"), sem("decay_exps_made")
        s_g = sem("chunk_products_done")
        s_at = sem("coupling_matrix_made")
        s_ap = sem("chunk_products_decayed")
        s_pair, s_pairT, s_invc = sem("pairs_inverted"), sem("pairs_turned"), sem("pairs_copied")
        s_ct, s_m1p, s_m1 = sem("coupling_made"), sem("coupling_product_done"), sem("coupling_product_copied")
        s_x, s_t = sem("join_products_done"), sem("blocks_joined")
        s_kx = sem("keys_decayed")
        s_qd = sem("queries_decayed")
        s_w, s_wn = sem("w_product_done"), sem("w_copied")
        s_zc = sem("z_activated")
        s_vnp, s_vn = sem("new_value_done"), sem("new_value_copied")
        s_kdp, s_state = sem("chunk_output_done"), sem("state_updated")
        s_sqo, s_sso, s_stdo = sem("output_squares_made"), sem("output_squares_summed"), sem("output_deviation")
        s_on, s_oT, s_og, s_ost = sem("output_normed"), sem("output_turned"), sem("output_gated"), sem("output_stored")
        L = 2 * len(LEVELS)

        def peeled(h):
            return isinstance(h, int) and h == 0

        block = ctx.enter_context(nc.Block())

        def heads(engine, body, after):
            body(0)
            with engine.Fori(1, H) as h:
                body(h)
            after(H)

        @block.sync
        def _(sp):
            sp.dma_start(taps[:, :, :], conv_w).then_inc(s_taps, 16)
            sp.dma_start(gain[:, :], o_gain).then_inc(s_taps, 16)

            def load(n, k):
                sp.dma_start(raw[k % SLOTS][:, :], w_in[bass.ds(n, 1), :, :].rearrange("a p f -> p (a f)")) \
                    .then_inc(s_raw[k % SLOTS], 16)

            def store(h):
                sp.wait_ge(s_og, h + 1)
                sp.dma_start(mixed[bass.ds(h, 1), :, :].rearrange("a p t -> p (a t)"), og[:, :]) \
                    .then_inc(s_ost, 16)

            load(0, 0)
            load(1, 1)

            def body(h):
                for k in range(SLOTS, 4 + SLOTS):
                    sp.wait_ge(s_lo, 4 * h + k - SLOTS + 1)
                    load(4 * h + k if isinstance(h, int) else (4 * h + k) % (4 * H), k)
                if not peeled(h):
                    store(h - 1)

            heads(sp, body, lambda h: store(h - 1))
            sp.wait_ge(s_ost, 16 * H)

        @block.gpsimd
        def _(pool):
            for i in range(2):
                pool.memset(u[i][:, 0:pad], 0.0)
            pool.drain().then_inc(s_set, 1)

            def split(h, k):
                pool.wait_ge(s_hi, 4 * h + k + 1)
                s = k % SLOTS
                pool.tensor_tensor(w_lo[s][:, :], raw[s][:, :], w_hi[s][:, :].bitcast(F32), ALU.subtract) \
                    .then_inc(s_lo, 1)

            def coupling(h, n):
                if n == 0:
                    pool.wait_ge(s_at, h + 1)
                elif n == 1:
                    pool.wait_ge(s_qd, h + 1)
                else:
                    pool.wait_ge(s_m1p, L * h + 2 * (n - 1))
                pool.tensor_tensor(cT[n % 2][:, :, :], aT[:, :, :], each(masks[:, n + 1, :]), ALU.mult) \
                    .then_inc(s_ct, 1)

            split(0, 0)
            split(0, 1)

            def body(h):
                split(h, 2)
                split(h, 3)
                split(h, 4)
                pool.wait_ge(s_ft, 3 * h + 1)
                pool.wait_ge(s_nrm, 4 * h + 3)
                pool.tensor_tensor(kn[:, :, :], kn[:, :, :], wide(hg[:, G_TO_END, :]), ALU.mult).then_inc(s_kx, 1)
                pool.wait_ge(s_ft, 3 * h + 2)
                pool.tensor_tensor(kb[:, :, :], kb[:, :, :], wide(hg[:, G_CUM_EXP, :]), ALU.mult).then_inc(s_kx, 1)
                coupling(h, 0)
                coupling(h, 1)
                split(h, 5)
                for n in range(2, len(LEVELS)):
                    coupling(h, n)

            heads(pool, body, lambda h: None)

        @block.scalar
        def _(act):
            def high(h, k):
                act.wait_ge(s_raw[k % SLOTS], 16 * (2 * h + k // 2) + 16)
                if not (peeled(h) and k < SLOTS):
                    act.wait_ge(s_a, 8 * h + 2 * (k - SLOTS) + 2)
                act.activation(w_hi[k % SLOTS][:, :], raw[k % SLOTS][:, :], ACT.Copy).then_inc(s_hi, 1)

            def evict(h, k):
                for half in range(2):
                    act.wait_ge(s_a, 8 * h + 2 * k + half + 1)
                    cols = slice(half * HALF, (half + 1) * HALF)
                    out = z[:, cols] if k == 3 else u[k % 2][:, pad + half * HALF:pad + (half + 1) * HALF]
                    act.activation(out, pa[:, cols], ACT.Copy).then_inc(s_u, 1)

            def silu(h, k):
                act.wait_ge(s_conv, 3 * h + k + 1)
                act.activation(qkv[k][:, :], qkv[k][:, :], ACT.Silu).then_inc(s_silu, 1)

            def project(h):
                if not peeled(h):
                    act.wait_ge(s_conv, 3 * h)
                evict(h, 0)
                high(h, 2)
                act.wait_ge(s_dm, h + 1)
                act.activation(decay[:, :, :], decay[:, :, :], ACT.Exp).then_inc(s_dx, 1)
                act.activation(from_start[:, :, :], by_chunk(pm), ACT.Exp).then_inc(s_dx, 1)
                evict(h, 1)
                high(h, 3)
                silu(h, 0)
                evict(h, 2)
                high(h, 4)
                silu(h, 1)

            def output_squares(h):
                act.wait_ge(s_kdp, 8 * h + 8)
                act.activation(on[:, :, :], by_chunk(pt), ACT.Square).then_inc(s_sqo, 1)

            def output_deviation(h):
                act.wait_ge(s_sso, h + 1)
                act.activation(stdo[:, :], sso[:, :], ACT.Sqrt, scale=1.0 / P, bias=eps[:, 0:1]) \
                    .then_inc(s_stdo, 1)

            def prepare(h):
                if not peeled(h):
                    output_squares(h - 1)
                act.wait_ge(s_tok, 3 * h + 1)
                act.activation(aT[:, :, :], by_chunk(pm), ACT.Square).then_inc(s_sq, 1)
                act.wait_ge(s_tok, 3 * h + 2)
                act.activation(attn[:, :, :], by_chunk(pt, T), ACT.Square).then_inc(s_sq, 1)
                act.wait_ge(s_ss, h + 1)
                act.activation(std[:, :], ss[:, :], ACT.Sqrt, bias=eps[:, 0:1]).then_inc(s_std, 1)
                if not peeled(h):
                    output_deviation(h - 1)
                silu(h, 2)
                for n, (out, psum) in enumerate(((knT[:, :, :], by_chunk(pm)), (kqT[:, :, 0:P], by_chunk(pm)),
                                                 (kqT[:, :, P:2 * P], by_chunk(pt)))):
                    act.wait_ge(s_ft, 3 * h + n + 1)
                    act.activation(out, psum, ACT.Copy).then_inc(s_kq, 1)
                evict(h, 3)
                high(h, 5)
                act.wait_ge(s_pairT, h + 1)
                act.activation(inv[:, :, :], by_chunk(pm), ACT.Copy).then_inc(s_invc, 1)
                for n in range(L):
                    part = slice(n % 2 * 4, n % 2 * 4 + 4)
                    act.wait_ge(s_m1p, L * h + n + 1)
                    if n < L - 2:
                        out, psum = m1[:, part, :], by_chunk(pm)[:, part, :]
                    else:
                        out, psum = m1[:, part, 0:P // 2], by_chunk(pm)[:, part, 0:P // 2]
                    act.activation(out, psum, ACT.Copy).then_inc(s_m1, 1)
                act.wait_ge(s_w, h + 1)
                act.activation(wTn[:, :, :], by_chunk(pm), ACT.Copy, scale=-1.0).then_inc(s_wn, 1)
                if not peeled(h):
                    act.wait_ge(s_og, h)
                act.activation(zc[:, :], z[:, :], ACT.Silu).then_inc(s_zc, 1)

            high(0, 0)
            high(0, 1)

            def body(h):
                project(h)
                prepare(h)

            heads(act, body, lambda h: (output_squares(h - 1), output_deviation(h - 1)))

        @block.vector
        def _(dve):
            def conv_taps(h, k, some):
                x, src = qkv[k], u[k % 2]
                w = taps[:, bass.ds(3 * h + k, 1), :]
                for n in some:
                    tap = pad - n
                    dve.drain()
                    if n == 0:
                        dve.wait_ge(s_u, 8 * h + 2 * k + 2)
                        if not peeled(h):
                            dve.wait_ge(s_tok, 3 * h)
                        dve.tensor_scalar(x[:, :], src[:, tap:tap + T], w[:, 0, tap:tap + 1], None, ALU.mult)
                    else:
                        ins = dve.scalar_tensor_tensor(out=x[:, :], in0=src[:, tap:tap + T],
                                                       scalar=w[:, 0, tap:tap + 1], in1=x[:, :],
                                                       op0=ALU.mult, op1=ALU.add)
                        if n == pad:
                            ins.then_inc(s_conv, 1)

            def new_value(h, c):
                dve.wait_ge(s_vnp, 8 * h + c + 1)
                dve.tensor_copy(vn[c % 2][:, :], pt[:, T:T + P]).then_inc(s_vn, 1)

            def update_state(h, c):
                added = pt[:, T + HALF:T + HALF + P]
                dve.drain()
                dve.wait_ge(s_kdp, 8 * h + c + 1)
                if c == 0:
                    dve.tensor_copy(state[:, :], added).then_inc(s_state, 1)
                else:
                    dve.scalar_tensor_tensor(out=state[:, :], in0=state[:, :], scalar=chunk_decay[:, c:c + 1],
                                             in1=added, op0=ALU.mult, op1=ALU.add).then_inc(s_state, 1)

            def head_decay(h):
                dve.wait_ge(s_gcb, h + 1)
                dve.tensor_tensor(decay[:, :, :], by_chunk(pm), wide(hg[:, G_CUM, :]), ALU.subtract)
                dve.drain()
                dve.tensor_scalar(decay[:, :, :], decay[:, :, :], 0.0, None, ALU.min).then_inc(s_dm, 1)

            def mask_decay(h):
                dve.wait_ge(s_dx, 2 * h + 1)
                dve.tensor_tensor(decay[:, :, :], decay[:, :, :], each(upper[:, :]), ALU.mult)

            def project_and_scan(h, projects, scans):
                beside = {}
                if projects:
                    dve.drain()
                    if not peeled(h):
                        dve.wait_ge(s_kx, 2 * h)
                    dve.tensor_copy(hg[:, :, :].unsqueeze(1), gates[:, bass.ds(h, 1), :, :])
                    dve.drain()
                    dve.tensor_copy(m1[:, :, :], wide(hg[:, G_LOG, :])).then_inc(s_gb, 1)
                    beside = {1: lambda: head_decay(h), 3: lambda: conv_taps(h, 0, (0, 1)),
                              4: lambda: conv_taps(h, 0, (2, 3)), 5: lambda: mask_decay(h),
                              6: lambda: conv_taps(h, 1, (0, 1)), 7: lambda: conv_taps(h, 1, (2, 3))}
                for n in range(NT):
                    if scans:
                        new_value(h - 1, n)
                    if n in beside:
                        beside[n]()
                    if scans and n < NT - 1:
                        update_state(h - 1, n)

            def output_sums(h):
                dve.wait_ge(s_sqo, h + 1)
                dve.tensor_reduce(out=sso[:, :], in_=on[:, :, :], axis=AX_X, op=ALU.add).then_inc(s_sso, 1)

            def output_norm(h):
                dve.wait_ge(s_stdo, h + 1)
                dve.reciprocal(rso[:, :], stdo[:, :])
                dve.drain()
                dve.tensor_tensor(on[:, :, :], by_chunk(pt), wide(rso[:, :]), ALU.mult).then_inc(s_on, 1)

            def output_gate(h):
                dve.wait_ge(s_zc, h + 1)
                if not (isinstance(h, int) and h == 0):
                    dve.wait_ge(s_ost, 16 * h)
                dve.wait_ge(s_oT, h + 1)
                dve.scalar_tensor_tensor(out=og[:, :], in0=pt[:, T:2 * T], scalar=gain[:, 0:1], in1=zc[:, :],
                                         op0=ALU.mult, op1=ALU.mult).then_inc(s_og, 1)

            def prepare(h):
                conv_taps(h, 2, (0, 1))
                dve.wait_ge(s_sq, 2 * h + 1)
                dve.tensor_reduce(out=ss[:, 0:NT], in_=aT[:, :, :], axis=AX_X, op=ALU.add)
                dve.wait_ge(s_sq, 2 * h + 2)
                dve.tensor_reduce(out=ss[:, NT:2 * NT], in_=attn[:, :, :], axis=AX_X, op=ALU.add)
                dve.drain().then_inc(s_ss, 1)
                if not peeled(h):
                    output_sums(h - 1)
                conv_taps(h, 2, (2, 3))
                dve.wait_ge(s_std, h + 1)
                dve.reciprocal(rs[:, :], std[:, :])
                dve.drain()
                dve.tensor_scalar(rs[:, NT:2 * NT], rs[:, NT:2 * NT], float(P) ** -0.5, None, ALU.mult)
                dve.tensor_tensor(kn[:, :, :], by_chunk(pm), wide(rs[:, 0:NT]), ALU.mult).then_inc(s_nrm, 1)
                dve.drain()
                dve.tensor_tensor(qn[:, :, :], by_chunk(pt, T), wide(rs[:, NT:2 * NT]), ALU.mult).then_inc(s_nrm, 1)
                if not peeled(h):
                    output_norm(h - 1)
                dve.tensor_tensor(kb[:, :, :], kn[:, :, :], wide(hg[:, G_BETA, :]), ALU.mult).then_inc(s_nrm, 1)
                dve.tensor_copy(chunk_decay[:, :], hg[:, G_CHUNK, :])
                dve.wait_ge(s_tok, 3 * h + 3)
                dve.tensor_tensor(vb[:, :, :], by_chunk(pt), wide(hg[:, G_BETA, :]), ALU.mult).then_inc(s_nrm, 1)
                if not peeled(h):
                    output_gate(h - 1)
                dve.wait_ge(s_g, h + 1)
                products = pt[:, :].rearrange("p (c t) -> p c t", c=NT)
                dve.tensor_tensor(aT[:, :, :], products[:, :, 0:P], decay[:, :, :], ALU.mult).then_inc(s_at, 1)
                dve.drain()
                dve.tensor_tensor(invT[:, :, :], aT[:, :, :], each(masks[:, 0, :]), ALU.mult)
                dve.drain()
                dve.tensor_tensor(invT[:, :, :], each(ident[:, :]), invT[:, :, :], ALU.subtract).then_inc(s_pair, 1)
                dve.tensor_tensor(attn[:, :, :], products[:, :, P:2 * P], decay[:, :, :], ALU.mult).then_inc(s_ap, 1)
                dve.wait_ge(s_kq, 3 * h + 3)
                dve.tensor_tensor(qdT[:, :, :], kqT[:, :, P:2 * P], from_start[:, :, :], ALU.mult).then_inc(s_qd, 1)
                for n in range(len(LEVELS)):
                    last = n == len(LEVELS) - 1
                    for a in range(2):
                        part = slice(a * 4, a * 4 + 4)
                        dve.drain()
                        if n == 0 and a == 0:
                            dve.wait_ge(s_invc, h + 1)
                        dve.wait_ge(s_x, L * h + 2 * n + a + 1)
                        x = pt[:, a * T:(a + 1) * T].rearrange("p (m c t) -> p m c t", m=2, c=4)
                        if last:
                            low, high = slice(0, P // 2), slice(P // 2, P)
                            dve.tensor_tensor(invT[low, part, high], invT[low, part, high], x[low, 1, :, high],
                                              ALU.subtract).then_inc(s_t, 1)
                            continue
                        dve.tensor_tensor(inv[:, part, :], inv[:, part, :], x[:, 0], ALU.subtract)
                        dve.tensor_tensor(invT[:, part, :], invT[:, part, :], x[:, 1], ALU.subtract) \
                            .then_inc(s_t, 1)

            dve.wait_ge(s_taps, 32)
            dve.wait_ge(s_set, 1)

            def body(h):
                project_and_scan(h, True, not peeled(h))
                prepare(h)

            heads(dve, body, lambda h: (project_and_scan(h, False, True), output_sums(h - 1),
                                        output_norm(h - 1), output_gate(h - 1)))

        @block.tensor
        def _(pe):
            def project_part(h, n):
                k, half, part = n // 4, n // 2 % 2, n % 2
                s = k % SLOTS
                cols = slice(half * HALF, (half + 1) * HALF)
                if part == 0:
                    pe.wait_ge(s_lo, 4 * h + k + 1)
                    if not (peeled(h) and n < 4):
                        pe.wait_ge(s_u, 8 * h + n // 2 - 1)
                for kt in range(part * KT // 2, (part + 1) * KT // 2):
                    f = slice(kt * P, (kt + 1) * P)
                    last = product3(pe, pa[:, cols], w_hi[s][:, f], w_lo[s][:, f], x_hi[:, kt, cols],
                                    x_lo[:, kt, cols], kt == 0, kt == KT - 1)
                if part == 1:
                    last.then_inc(s_a, 1)

            def scan_value(h, c):
                out = pt[:, T:T + P]
                if c == 0:
                    pe.matmul(out, invT[:, c, :], vb[:, c, :], start=True, stop=True).then_inc(s_vnp, 1)
                    return
                pe.matmul(out, invT[:, c, :], vb[:, c, :], start=True, stop=False)
                if c == 1:
                    pe.wait_ge(s_wn, h + 1)
                pe.wait_ge(s_state, 7 * h + c)
                pe.matmul(out, wTn[:, c, :], state[:, :], start=False, stop=True).then_inc(s_vnp, 1)

            def scan_output(h, c):
                out = pt[:, c * P:(c + 1) * P]
                if c:
                    pe.matmul(out, qdT[:, c, :], state[:, :], start=True, stop=False)
                pe.wait_ge(s_vn, 8 * h + c + 1)
                last = pe.matmul(out, attn[:, c, :], vn[c % 2][:, :], start=c == 0, stop=True)
                if c < NT - 1:
                    last = pe.matmul(pt[:, T + HALF:T + HALF + P], kn[:, c, :], vn[c % 2][:, :],
                                     start=True, stop=True)
                last.then_inc(s_kdp, 1)

            def decay_by_columns(h):
                pe.wait_ge(s_gb, h + 1)
                if not peeled(h):
                    pe.wait_ge(s_wn, h)
                for c in range(NT):
                    last = pe.matmul(pm[:, c * P:(c + 1) * P], m1[:, c, :], upper[:, :], start=True, stop=True)
                last.then_inc(s_gcb, 1)

            def turn(out, source):
                for c in range(NT):
                    last = pe.transpose(out[:, c, :], source[:, c, :], ident[:, :])
                return last

            def output_turn(h):
                turn(by_chunk(pt, T), on).then_inc(s_oT, 1)

            def prepare(h):
                def heads_of(x):
                    return x[:, :].rearrange("p (c t) -> p c t", c=NT)

                pe.wait_ge(s_silu, 3 * h + 2)
                pe.wait_ge(s_dx, 2 * h + 2)
                turn(by_chunk(pm), heads_of(qkv[1])).then_inc(s_tok, 1)
                if not peeled(h):
                    pe.wait_ge(s_state, 7 * h)
                turn(by_chunk(pt, T), heads_of(qkv[0])).then_inc(s_tok, 1)
                project_part(h, 12)
                project_part(h, 13)
                pe.wait_ge(s_nrm, 4 * h + 1)
                turn(by_chunk(pm), kn).then_inc(s_ft, 1)
                if not peeled(h):
                    pe.wait_ge(s_on, h)
                pe.wait_ge(s_silu, 3 * h + 3)
                turn(by_chunk(pt), heads_of(qkv[2])).then_inc(s_tok, 1)
                pe.wait_ge(s_nrm, 4 * h + 3)
                if not peeled(h):
                    output_turn(h - 1)
                pe.wait_ge(s_kq, 3 * h + 1)
                turn(by_chunk(pm), kb).then_inc(s_ft, 1)
                project_part(h, 14)
                pe.wait_ge(s_nrm, 4 * h + 4)
                turn(by_chunk(pt), qn).then_inc(s_ft, 1)
                if not peeled(h):
                    pe.wait_ge(s_og, h)
                pe.wait_ge(s_kq, 3 * h + 3)
                for c in range(NT):
                    last = pe.matmul(pt[:, c * 2 * P:(c + 1) * 2 * P], knT[:, c, :], kqT[:, c, :],
                                     start=True, stop=True)
                last.then_inc(s_g, 1)
                project_part(h, 15)
                pe.wait_ge(s_pair, h + 1)
                turn(by_chunk(pm), invT).then_inc(s_pairT, 1)
                pe.wait_ge(s_invc, h + 1)
                pe.wait_ge(s_ap, h + 1)
                for n in range(len(LEVELS)):
                    final = n == len(LEVELS) - 1
                    c_level = cT[n % 2]
                    low, high = slice(0, P // 2), slice(P // 2, P)
                    pe.wait_ge(s_ct, 6 * h + n + 1)
                    for a in range(2):
                        if n:
                            pe.wait_ge(s_t, L * h + 2 * n - 1 + a)
                        for c in range(4 * a, 4 * a + 4):
                            out = by_chunk(pm)[:, c, :]
                            if final:
                                last = pe.matmul(out[:, low], c_level[:, c, :], inv[:, c, low],
                                                 start=True, stop=True)
                            else:
                                last = pe.matmul(out, c_level[:, c, :], inv[:, c, :], start=True, stop=True)
                        last.then_inc(s_m1p, 1)
                    for a in range(2):
                        pe.wait_ge(s_m1, L * h + 2 * n + a + 1)
                        for c in range(4):
                            at = a * T + c * P
                            i = 4 * a + c
                            if final:
                                last = pe.matmul(pt[:, at + HALF + P // 2:at + HALF + P], m1[:, i, :],
                                                 invT[:, i, high], start=True, stop=True)
                                continue
                            pe.matmul(pt[:, at:at + P], invT[:, i, :], m1[:, i, :], start=True, stop=True)
                            last = pe.matmul(pt[:, at + HALF:at + HALF + P], m1[:, i, :], invT[:, i, :],
                                             start=True, stop=True)
                        last.then_inc(s_x, 1)
                pe.wait_ge(s_t, L * h + L)
                pe.wait_ge(s_kx, 2 * h + 2)
                pe.wait_ge(s_qd, h + 1)
                for c in range(NT):
                    last = pe.matmul(pm[:, c * P:(c + 1) * P], kb[:, c, :], invT[:, c, :], start=True, stop=True)
                last.then_inc(s_w, 1)

            def body(h):
                n = 0
                for c in range(NT):
                    if not peeled(h):
                        scan_value(h - 1, c)
                    project_part(h, n)
                    n += 1
                    if not peeled(h):
                        scan_output(h - 1, c)
                    if c % 2 == 0:
                        project_part(h, n)
                        n += 1
                    if c == 0:
                        decay_by_columns(h)
                prepare(h)

            def after(h):
                for n in range(NT):
                    scan_value(h - 1, n)
                    scan_output(h - 1, n)
                pe.wait_ge(s_on, h)
                output_turn(h - 1)

            heads(pe, body, after)


GLA_HEADS = 4
GLA_DK = 128
GLA_DV = 256
GLA_RANK = 16
GLA_TILES = 6
GLA_TAU = 16.0


def gla_gates(nc, consts, w_small, w_up, bias, x_hi, x_lo, cum):
    ctx = ExitStack()
    with ctx:
        sb, ps = buffers(nc, ctx)
        sem = semaphores(nc, ctx, "la_")
        raw = sb("la_raw", [P, KT, GLA_RANK])
        w_hi = sb("la_whi", [P, KT, GLA_RANK], F32R)
        w_lo = sb("la_wlo", [P, KT, GLA_RANK], F32R)
        logits = ps("la_logits", [P, NT, GLA_RANK])
        low = sb("la_low", [P, NT, GLA_RANK])
        lowT = sb("la_lowT", [GLA_RANK, T])
        up = sb("la_up", [GLA_RANK, GLA_HEADS * P])
        b = sb("la_bias", [P, GLA_HEADS])
        keep = sb("la_keep", [P, NT, P])
        y, a = (sb(f"la_{x}", [P, T]) for x in "ya")
        turned = ps("la_turned", [GLA_RANK, T])
        full = [ps(f"la_full{i}", [P, T]) for i in range(2)]
        s_in = sem("gains_loaded")
        s_low = sem("gate_input_made")
        s_turn = sem("gate_turned")
        s_lowT = sem("gate_turned_copied")
        s_full = sem("gate_full_done")
        s_y = sem("gate_biased")
        s_abs = sem("gate_absolute_made")
        s_ln = sem("gate_exps_made")
        s_raw, s_hi, s_lo = sem("w_raw"), sem("w_high"), sem("w_low")
        s_done = sem("gate_logits_done")
        block = ctx.enter_context(nc.Block())

        @block.sync
        def _(sp):
            sp.dma_start(raw[:, :, :], w_small).then_inc(s_raw, 16)
            sp.dma_start(up[:, :], w_up).then_inc(s_in, 16)
            sp.dma_start(b[:, :], bias).then_inc(s_in, 16)

        @block.scalar
        def _(act):
            act.wait_ge(s_raw, 16)
            act.activation(w_hi[:, :, :], raw[:, :, :], ACT.Copy).then_inc(s_hi, 1)
            for h in range(GLA_HEADS):
                act.wait_ge(s_abs, h + 1)
                act.activation(a[:, :], a[:, :], ACT.Exp, scale=-1.0)
                act.drain()
                act.activation(a[:, :], a[:, :], ACT.Ln, bias=consts["ones"][:, 0:1]).then_inc(s_ln, 1)

        @block.vector
        def _(dve):
            dve.wait_ge(s_hi, 1)
            dve.tensor_tensor(w_lo[:, :, :], raw[:, :, :], w_hi[:, :, :].bitcast(F32), ALU.subtract) \
                .then_inc(s_lo, 1)
            dve.memset(keep[:, :, :], 1.0)
            dve.drain()
            dve.memset(keep[:, :, 0:1], 0.0)
            dve.wait_ge(s_done, 1)
            dve.tensor_copy(low[:, :, :], logits[:, :, :]).then_inc(s_low, 1)
            dve.wait_ge(s_turn, 1)
            dve.tensor_copy(lowT[:, :], turned[:, :]).then_inc(s_lowT, 1)
            dve.wait_ge(s_in, 32)
            for h in range(GLA_HEADS):
                dve.wait_ge(s_full, h + 1)
                dve.drain()
                dve.tensor_scalar(y[:, :], full[h % 2][:, :], b[:, h:h + 1], None, ALU.add).then_inc(s_y, 1)
                dve.drain()
                dve.scalar_tensor_tensor(out=a[:, :], in0=y[:, :], scalar=-1.0, in1=y[:, :], op0=ALU.mult,
                                         op1=ALU.max).then_inc(s_abs, 1)
                dve.wait_ge(s_ln, h + 1)
                dve.scalar_tensor_tensor(out=y[:, :], in0=y[:, :], scalar=0.0, in1=a[:, :], op0=ALU.min,
                                         op1=ALU.subtract)
                dve.drain()
                dve.tensor_tensor_scan(out=a[:, :], data0=keep[:, :, :].rearrange("p c t -> p (c t)"),
                                       data1=y[:, :], initial=0.0, op0=ALU.mult, op1=ALU.add)
                dve.drain()
                dve.tensor_scalar(cum[:, h, :], a[:, :], 1.0 / GLA_TAU, None, ALU.mult)

        @block.tensor
        def _(pe):
            pe.wait_ge(s_lo, 1)
            token_logits(pe, logits, x_hi, x_lo, w_hi, w_lo).then_inc(s_done, 1)
            pe.wait_ge(s_low, 1)
            for c in range(NT):
                last = pe.matmul(turned[:, c * P:(c + 1) * P], low[:, c, :], consts["ident"][:, :],
                                 start=True, stop=True)
            last.then_inc(s_turn, 1)
            pe.wait_ge(s_lowT, 1)
            pe.wait_ge(s_in, 32)
            for h in range(GLA_HEADS):
                if h >= 2:
                    pe.wait_ge(s_y, h - 1)
                for half in range(2):
                    cols = slice(half * HALF, (half + 1) * HALF)
                    last = pe.matmul(full[h % 2][:, cols], up[:, h * P:(h + 1) * P], lowT[:, cols],
                                     start=True, stop=True)
                last.then_inc(s_full, 1)


def gla(nc, consts, w_in, o_gain, cum, x_hi, x_lo, mixed):
    ident, eps, masks = consts["ident"], consts["eps"], consts["masks"]
    sizes = (64, 32, 16, 8, 4, 2, 1)
    N = len(sizes)
    ctx = ExitStack()
    with ctx:
        sb, ps = buffers(nc, ctx)
        sem = semaphores(nc, ctx, "l_")
        H = GLA_HEADS
        raw = [sb(f"l_raw{i}", [P, D]) for i in range(SLOTS)]
        w_hi = [sb(f"l_whi{i}", [P, D], F32R) for i in range(SLOTS)]
        w_lo = [sb(f"l_wlo{i}", [P, D], F32R) for i in range(SLOTS)]
        qT, kT, bh, attn, tmp, qd, kd = (sb("l_" + x, [P, T]) for x in ("qT", "kT", "bh", "attn", "tmp", "qd", "kd"))
        vT, r, rc, og, ex = ([sb(f"l_{x}{i}", [P, T]) for i in range(2)] for x in ("vT", "r", "rc", "og", "ex"))
        kt = sb("l_kt", [P, NT, P])
        v = sb("l_v", [P, NT, GLA_DV])
        on = sb("l_on", [P, NT, GLA_DV])
        state = [sb(f"l_state{i}", [P, GLA_DV]) for i in range(2)]
        cd = sb("l_cd", [P, NT])
        sso, stdo, rso = (sb(f"l_{x}", [P, NT]) for x in ("sso", "stdo", "rso"))
        gain = sb("l_gain", [P, 2])
        pa = ps("l_pa", [P, T])
        pm = ps("l_pm", [P, T])
        pt = ps("l_pt", [P, 2 * T])

        def by_chunk(x):
            return x[:, :].rearrange("p (c t) -> p c t", c=NT)

        s_raw = [sem(f"w_raw{i}") for i in range(SLOTS)]
        s_hi, s_lo = sem("w_high"), sem("w_low")
        s_taps = sem("taps_loaded")
        s_a, s_u = sem("projection_half_done"), sem("projection_half_evicted")
        s_b = sem("log_decay_repeated")
        s_sub, s_exp, s_f = sem("level_exponent_made"), sem("level_exps_made"), sem("level_factors_made")
        s_lp, s_lacc = sem("level_product_done"), sem("level_product_added")
        s_end, s_endx = sem("decay_exponent_made"), sem("decay_exps_made")
        s_qk = sem("keys_decayed")
        s_prep = sem("chunk_products_decayed")
        s_ktp, s_kt = sem("feature_major_in_psum"), sem("feature_major_made")
        s_vp, s_v = sem("token_major_in_psum"), sem("normed")
        s_rc = sem("z_activated")
        s_kdp, s_o, s_state = sem("new_value_done"), sem("chunk_output_done"), sem("state_updated")
        s_sqo, s_sso, s_stdo = sem("output_squares_made"), sem("output_squares_summed"), sem("output_deviation")
        s_on, s_oT, s_og, s_ost = sem("output_normed"), sem("output_turned"), sem("output_gated"), sem("output_stored")

        def peeled(h):
            return isinstance(h, int) and h == 0

        block = ctx.enter_context(nc.Block())

        def heads(engine, body, after):
            body(0)
            with engine.Fori(1, H) as h:
                body(h)
            after(H)

        @block.sync
        def _(sp):
            sp.dma_start(gain[:, :], o_gain).then_inc(s_taps, 16)

            def store(h):
                for j in range(2):
                    sp.wait_ge(s_og, 2 * h + j + 1)
                    sp.dma_start(mixed[bass.ds(2 * h + j, 1), :, :].rearrange("a p t -> p (a t)"), og[j][:, :]) \
                        .then_inc(s_ost, 16)

            def body(h):
                for k in range(GLA_TILES):
                    if not (peeled(h) and k < SLOTS):
                        sp.wait_ge(s_lo, GLA_TILES * h + k - SLOTS + 1)
                    sp.dma_start(raw[k % SLOTS][:, :],
                                 w_in[bass.ds(GLA_TILES * h + k, 1), :, :].rearrange("a p f -> p (a f)")) \
                        .then_inc(s_raw[k % SLOTS], 16)
                if not peeled(h):
                    store(h - 1)

            heads(sp, body, lambda h: store(h - 1))
            sp.wait_ge(s_ost, 32 * H)

        @block.gpsimd
        def _(pool):
            def body(h):
                for k in range(GLA_TILES):
                    pool.wait_ge(s_hi, GLA_TILES * h + k + 1)
                    s = k % SLOTS
                    pool.tensor_tensor(w_lo[s][:, :], raw[s][:, :], w_hi[s][:, :].bitcast(F32), ALU.subtract) \
                        .then_inc(s_lo, 1)

            heads(pool, body, lambda h: None)

        @block.scalar
        def _(act):
            def high(h, k):
                act.wait_ge(s_raw[k % SLOTS], 16 * (3 * h + k // 2) + 16)
                if not (peeled(h) and k < SLOTS):
                    act.wait_ge(s_a, 12 * h + 2 * (k - SLOTS) + 2)
                act.activation(w_hi[k % SLOTS][:, :], raw[k % SLOTS][:, :], ACT.Copy).then_inc(s_hi, 1)

            def project(h):
                high(h, 0)
                high(h, 1)
                act.drain()
                if not peeled(h):
                    act.wait_ge(s_prep, h)
                for k, out in enumerate((qT, kT, *vT, *r)):
                    for half in range(2):
                        act.wait_ge(s_a, 12 * h + 2 * k + half + 1)
                        cols = slice(half * HALF, (half + 1) * HALF)
                        act.activation(out[:, cols], pa[:, cols], ACT.Copy,
                                       scale=float(GLA_DK) ** -0.5 if k == 0 else 1.0).then_inc(s_u, 1)
                    if k < GLA_TILES - 2:
                        high(h, k + 2)

            def output_squares(h):
                act.wait_ge(s_o, 8 * h + 8)
                act.activation(on[:, :, :], pt[:, :].rearrange("p (c d) -> p c d", c=NT), ACT.Square) \
                    .then_inc(s_sqo, 1)
                act.wait_ge(s_sso, h + 1)
                act.activation(stdo[:, :], sso[:, :], ACT.Sqrt, scale=1.0 / GLA_DV, bias=eps[:, 0:1]) \
                    .then_inc(s_stdo, 1)

            def prepare(h):
                for n, s in enumerate(sizes):
                    act.wait_ge(s_sub, N * h + n + 1)
                    e = ex[n % 2][:, :].rearrange("p (b half t) -> p b half t", half=2, t=s)
                    act.activation(e[:, :, 0, :], e[:, :, 0, :], ACT.Exp, scale=-1.0)
                    act.activation(e[:, :, 1, :], e[:, :, 1, :], ACT.Exp)
                    act.drain().then_inc(s_exp, 1)
                act.wait_ge(s_end, h + 1)
                act.activation(qd[:, :], bh[:, :], ACT.Exp)
                act.activation(kd[:, :], kd[:, :], ACT.Exp)
                act.activation(cd[:, :].unsqueeze(2), by_chunk(bh)[:, :, P - 1:P], ACT.Exp)
                act.drain().then_inc(s_endx, 1)
                act.wait_ge(s_ktp, h + 1)
                act.activation(kt[:, :, :], by_chunk(pm), ACT.Copy).then_inc(s_kt, 1)
                act.wait_ge(s_vp, h + 1)
                act.activation(v[:, :, :], pt[:, :].rearrange("p (c d) -> p c d", c=NT), ACT.Copy) \
                    .then_inc(s_v, 1)
                for j in range(2):
                    act.activation(rc[j][:, :], r[j][:, :], ACT.Silu)
                act.drain().then_inc(s_rc, 1)

            def body(h):
                project(h)
                if not peeled(h):
                    output_squares(h - 1)
                prepare(h)

            heads(act, body, lambda h: output_squares(h - 1))

        @block.vector
        def _(dve):
            def update_state(h, c):
                dve.drain()
                dve.wait_ge(s_kdp, 7 * h + c + 1)
                out, psum = state[(c + 1) % 2], pm[:, c % 2 * HALF:c % 2 * HALF + GLA_DV]
                if c == 0:
                    dve.tensor_copy(out[:, :], psum).then_inc(s_state, 1)
                    return
                dve.wait_ge(s_o, 8 * h + c)
                dve.scalar_tensor_tensor(out=out[:, :], in0=state[c % 2][:, :], scalar=cd[:, c:c + 1], in1=psum,
                                         op0=ALU.mult, op1=ALU.add).then_inc(s_state, 1)

            def level_exponent(h, n):
                s = sizes[n]
                b = bh[:, :].rearrange("p (b t) -> p b t", t=2 * s)
                middle = b[:, :, s - 1:s].to_broadcast([P, T // (2 * s), 2 * s])
                if n >= 2:
                    dve.wait_ge(s_lp, 8 * h + n)
                dve.tensor_tensor(ex[n % 2][:, :].rearrange("p (b t) -> p b t", t=2 * s), b, middle,
                                  ALU.subtract).then_inc(s_sub, 1)

            def level_factors(h, n):
                s = sizes[n]
                e, q, k = (x[:, :].rearrange("p (b half t) -> p b half t", half=2, t=s) for x in (ex[n % 2], qT, kT))
                dve.wait_ge(s_exp, N * h + n + 1)
                dve.tensor_tensor(e[:, :, 0, :], e[:, :, 0, :], k[:, :, 0, :], ALU.mult)
                dve.tensor_tensor(e[:, :, 1, :], e[:, :, 1, :], q[:, :, 1, :], ALU.mult)
                dve.drain().then_inc(s_f, 1)

            def level_add(h, m):
                psum = pm if m % 2 == 0 else pa
                if m == 0:
                    dve.wait_ge(s_lp, 8 * h + 1)
                    dve.tensor_tensor(by_chunk(attn), by_chunk(psum), each(ident[:, :]), ALU.mult) \
                        .then_inc(s_lacc, 1)
                    return
                mask = masks[:, N - m, :]
                dve.drain()
                dve.wait_ge(s_lp, 8 * h + m + 1)
                dve.tensor_tensor(by_chunk(tmp), by_chunk(psum), each(mask), ALU.mult).then_inc(s_lacc, 1)
                dve.drain()
                dve.tensor_tensor(attn[:, :], attn[:, :], tmp[:, :], ALU.add)

            def output_sums(h):
                dve.wait_ge(s_sqo, h + 1)
                dve.tensor_reduce(out=sso[:, :], in_=on[:, :, :], axis=AX_X, op=ALU.add).then_inc(s_sso, 1)

            def output_norm(h):
                dve.wait_ge(s_stdo, h + 1)
                dve.reciprocal(rso[:, :], stdo[:, :])
                dve.drain()
                dve.tensor_tensor(on[:, :, :], pt[:, :].rearrange("p (c d) -> p c d", c=NT),
                                  wide(rso[:, :], GLA_DV), ALU.mult).then_inc(s_on, 1)

            def output_gate(h):
                dve.wait_ge(s_rc, h + 1)
                if not (isinstance(h, int) and h == 0):
                    dve.wait_ge(s_ost, 32 * h)
                dve.wait_ge(s_oT, h + 1)
                for j in range(2):
                    dve.scalar_tensor_tensor(out=og[j][:, :], in0=pt[:, j * T:(j + 1) * T], scalar=gain[:, j:j + 1],
                                             in1=rc[j][:, :], op0=ALU.mult, op1=ALU.mult).then_inc(s_og, 1)

            def prepare(h):
                dve.drain()
                dve.tensor_copy(bh[:, :].unsqueeze(1), cum[:, bass.ds(h, 1), :])
                dve.drain()
                level_exponent(h, 0)
                b = by_chunk(bh)
                dve.tensor_tensor(by_chunk(kd), b[:, :, P - 1:P].to_broadcast([P, NT, P]), b, ALU.subtract) \
                    .then_inc(s_end, 1)
                if not peeled(h):
                    output_sums(h - 1)
                    output_norm(h - 1)
                level_add(h, 0)
                for n in range(N):
                    if n < N - 1:
                        dve.drain()
                        level_exponent(h, n + 1)
                    level_factors(h, n)
                    if n:
                        level_add(h, n)
                    if n == 4 and not peeled(h):
                        output_gate(h - 1)
                level_add(h, N)
                dve.wait_ge(s_endx, h + 1)
                dve.tensor_tensor(qd[:, :], qd[:, :], qT[:, :], ALU.mult)
                dve.tensor_tensor(kd[:, :], kd[:, :], kT[:, :], ALU.mult)
                dve.drain().then_inc(s_prep, 1)

            dve.wait_ge(s_taps, 16)

            def scan(h):
                for c in range(NT - 1):
                    update_state(h, c)

            def body(h):
                if not peeled(h):
                    scan(h - 1)
                prepare(h)

            heads(dve, body, lambda h: (scan(h - 1), output_sums(h - 1), output_norm(h - 1), output_gate(h - 1)))

        @block.tensor
        def _(pe):
            def project_half(h, n):
                k = n // 2
                s = k % SLOTS
                cols = slice(n % 2 * HALF, (n % 2 + 1) * HALF)
                pe.wait_ge(s_lo, GLA_TILES * h + k + 1)
                if not (peeled(h) and n < 2):
                    pe.wait_ge(s_u, 12 * h + n - 1)
                for kt_ in range(KT):
                    f = slice(kt_ * P, (kt_ + 1) * P)
                    last = product3(pe, pa[:, cols], w_hi[s][:, f], w_lo[s][:, f], x_hi[:, kt_, cols],
                                    x_lo[:, kt_, cols], kt_ == 0, kt_ == KT - 1)
                last.then_inc(s_a, 1)

            def scan_chunk(h, c):
                if c == 0:
                    pe.wait_ge(s_rc, h + 1)
                if c < NT - 1:
                    if c >= 2:
                        pe.wait_ge(s_state, 7 * h + c - 1)
                    pe.matmul(pm[:, c % 2 * HALF:c % 2 * HALF + GLA_DV], kt[:, c, :], v[:, c, :],
                              start=True, stop=True).then_inc(s_kdp, 1)
                out = pt[:, c * GLA_DV:(c + 1) * GLA_DV]
                if c:
                    pe.wait_ge(s_state, 7 * h + c)
                    pe.matmul(out, by_chunk(qd)[:, c, :], state[c % 2][:, :], start=True, stop=False)
                pe.matmul(out, by_chunk(attn)[:, c, :], v[:, c, :], start=c == 0, stop=True).then_inc(s_o, 1)

            def turn(out, source):
                for c in range(NT):
                    last = pe.transpose(out[:, c, :], source[:, c, :], ident[:, :])
                return last

            def output_turn(h):
                pe.wait_ge(s_on, h + 1)
                for j in range(2):
                    last = turn(pt[:, j * T:(j + 1) * T].rearrange("p (c t) -> p c t", c=NT),
                                on[:, :, j * P:(j + 1) * P])
                last.then_inc(s_oT, 1)

            def level_product(h, m):
                psum = pm if m % 2 == 0 else pa
                if m == 0:
                    pe.wait_ge(s_u, 12 * h + 12)
                    if not peeled(h):
                        pe.wait_ge(s_state, 7 * h)
                else:
                    pe.wait_ge(s_f, N * h + m)
                if m >= 2:
                    pe.wait_ge(s_lacc, 8 * h + m - 1)
                for c in range(NT):
                    e = ex[(m - 1) % 2]
                    a, b = (kT, qT) if m == 0 else (e, e)
                    last = pe.matmul(psum[:, c * P:(c + 1) * P], by_chunk(a)[:, c, :], by_chunk(b)[:, c, :],
                                     start=True, stop=True)
                last.then_inc(s_lp, 1)

            def prepare(h):
                for m in range(N + 1):
                    level_product(h, m)
                    if m == 2 and not peeled(h):
                        output_turn(h - 1)
                pe.wait_ge(s_prep, h + 1)
                turn(by_chunk(pm), by_chunk(kd)).then_inc(s_ktp, 1)
                if not peeled(h):
                    pe.wait_ge(s_og, 2 * h)
                for j in range(2):
                    last = turn(pt[:, :].rearrange("p (c d) -> p c d", c=NT)[:, :, j * P:(j + 1) * P],
                                by_chunk(vT[j]))
                last.then_inc(s_vp, 1)

            def body(h):
                for n in range(2 * GLA_TILES):
                    if not peeled(h) and n < NT:
                        scan_chunk(h - 1, n)
                    project_half(h, n)
                prepare(h)

            def after(h):
                for n in range(NT):
                    scan_chunk(h - 1, n)
                output_turn(h - 1)

            heads(pe, body, after)


def build_program(nc, x, gdn_w_in, gdn_w_gates, gdn_conv_w, gdn_a_log, gdn_dt_bias, gdn_o_gain, gdn_w_out,
                  gla_w_in, gla_w_low, gla_w_up, gla_bias, gla_o_gain, gla_w_out, mix_pre, mix_post, ffn_pre,
                  ffn_post, ffn_w_up, ffn_conv_w, ffn_w_down, out):
    x_mid = [nc.dram_tensor(f"x_mid{i}", (NT, P, D), F32, kind="Internal").ap() for i in range(3)]
    mixed = nc.dram_tensor("mixed", (KT, P, T), F32, kind="Internal").ap()
    with ExitStack() as ctx:
        consts = constants(nc, ctx)
        consts["any_gain"] = mix_pre[0]
        sb, _ = buffers(nc, ctx)
        x_hi = sb("x_hi", [P, KT, T], F32R)
        x_lo = sb("x_lo", [P, KT, T], F32R)

        def feed_forward(layer, x_in, x_out, pre_gain):
            with nc.sbuf_tensor(f"acc{layer}", [P, NT, D], F32) as acc:
                ffn(nc, layer, ffn_w_up, ffn_conv_w, ffn_w_down, x_hi, x_lo, acc)
                token_pass(nc, f"after_ffn{layer}", consts, x_in, x_out, ffn_post[layer:layer + 1, :], pre_gain,
                           x_hi, x_lo, acc=acc)

        token_pass(nc, "first", consts, x, None, None, mix_pre[0], x_hi, x_lo)
        with nc.sbuf_tensor("gdn_gates", [P, GDN_HEADS, GATE_KINDS, NT], F32) as gates:
            gdn_gates(nc, consts, gdn_w_gates, gdn_a_log, gdn_dt_bias, x_hi, x_lo, gates)
            gdn(nc, consts, gdn_w_in, gdn_conv_w, gdn_o_gain, gates, x_hi, x_lo, mixed)
        token_pass(nc, "after_gdn", consts, x, x_mid[0], mix_post[0:1, :], ffn_pre[0], x_hi, x_lo,
                   mixed=mixed, w_out=gdn_w_out)
        feed_forward(0, x_mid[0], x_mid[1], mix_pre[1])
        with nc.sbuf_tensor("gla_cum", [P, GLA_HEADS, T], F32) as cum:
            gla_gates(nc, consts, gla_w_low, gla_w_up, gla_bias, x_hi, x_lo, cum)
            gla(nc, consts, gla_w_in, gla_o_gain, cum, x_hi, x_lo, mixed)
        token_pass(nc, "after_gla", consts, x_mid[1], x_mid[2], mix_post[1:2, :], ffn_pre[1], x_hi, x_lo,
                   mixed=mixed, w_out=gla_w_out)
        feed_forward(1, x_mid[2], out, None)


def kernel(**inputs):
    import numpy as np
    import concourse.bacc as bacc
    from concourse.bass_utils import run_bass_kernel_spmd

    a = {name: np.asarray(value) for name, value in inputs.items()}

    def tiles(w):
        return w.reshape(KT, P, -1, P).transpose(2, 1, 0, 3).reshape(-1, P, D)

    def by_partition(v):
        return np.swapaxes(v.reshape(*v.shape[:-1], -1, P), -1, -2)

    gdn_w = a["gdn_w_in"][0]
    gdn_cols = 4 * GDN_HEADS * P
    gdn_tiles = tiles(gdn_w[:, :gdn_cols]).reshape(4, GDN_HEADS, P, D).transpose(1, 0, 2, 3).reshape(-1, P, D)
    gla_w = a["gla_w_in"][0]
    gla_cols = GLA_TILES * GLA_HEADS * P
    t = tiles(gla_w[:, :gla_cols])
    n = GLA_HEADS
    gla_tiles = np.stack([t[i] for h in range(n) for i in
                          (h, n + h, 2 * n + 2 * h, 2 * n + 2 * h + 1, 4 * n + 2 * h, 4 * n + 2 * h + 1)])
    taps = a["gdn_conv_w"][0].reshape(GDN_TAPS, 3, GDN_HEADS, P).transpose(3, 2, 1, 0)
    depth = a["ffn_w_up"].shape[0]
    arrays = {
        "x": a["x"].reshape(NT, P, D),
        "gdn_w_in": gdn_tiles,
        "gdn_w_gates": gdn_w[:, gdn_cols:].reshape(KT, P, -1).transpose(1, 0, 2),
        "gdn_conv_w": taps.reshape(P, 3 * GDN_HEADS, GDN_TAPS),
        "gdn_a_log": a["gdn_a_log"],
        "gdn_dt_bias": a["gdn_dt_bias"],
        "gdn_o_gain": by_partition(a["gdn_o_norm"][0]),
        "gdn_w_out": a["gdn_w_out"][0].reshape(KT, P, D),
        "gla_w_in": gla_tiles,
        "gla_w_low": gla_w[:, gla_cols:].reshape(KT, P, -1).transpose(1, 0, 2),
        "gla_w_up": a["gla_w_gate_up"][0],
        "gla_bias": by_partition(a["gla_gate_bias"][0]),
        "gla_o_gain": by_partition(a["gla_o_norm"][0]),
        "gla_w_out": a["gla_w_out"][0].reshape(KT, P, D),
        "mix_pre": by_partition(a["mix_pre_norm"]),
        "mix_post": a["mix_post_norm"],
        "ffn_pre": by_partition(a["ffn_pre_norm"]),
        "ffn_post": a["ffn_post_norm"],
        "ffn_w_up": np.stack([tiles(w) for w in a["ffn_w_up"]]),
        "ffn_conv_w": a["ffn_conv_w"].reshape(depth, FFN_TAPS, UP_TILES, P).transpose(0, 3, 2, 1),
        "ffn_w_down": a["ffn_w_down"].reshape(depth, FT, P, D),
    }
    arrays = {f"in_{name}": np.ascontiguousarray(value) for name, value in arrays.items()}
    nc = bacc.Bacc("TRN2", target_bir_lowering=False, num_devices=1)
    args = [nc.dram_tensor(name, value.shape, mybir.dt.from_np(value.dtype), kind="ExternalInput").ap()
            for name, value in arrays.items()]
    out = nc.dram_tensor("out", (NT, P, D), F32, kind="ExternalOutput").ap()
    build_program(nc, *args, out)
    result = run_bass_kernel_spmd(nc, [arrays], core_ids=[0])
    return result.results[0]["out"].reshape(1, T, D)
```

```python
from contextlib import ExitStack

import concourse.bass as bass
from concourse import mybir

P = 128
T = 1024
D = 1024
KT = D // P
NT = T // P
HALF = 512
EPS = 1e-6

F32 = mybir.dt.float32
F32R = mybir.dt.float32r
ACT = mybir.ActivationFunctionType
ALU = mybir.AluOpType
AX_X = mybir.AxisListType.X

D_FF = 2816
FT = D_FF // P
UP_TILES = 2 * FT
PAIR = 2
GROUPS = FT // PAIR
FFN_TAPS = 3
RING = 3


def buffers(nc, ctx):
    def sb(name, shape, dt=F32):
        return ctx.enter_context(nc.sbuf_tensor(name, shape, dt))

    def ps(name, shape, dt=F32):
        return ctx.enter_context(nc.psum_tensor(name, shape, dt))

    return sb, ps


def semaphores(nc, ctx, tag):
    made = []

    def sem(name):
        made.append(ctx.enter_context(nc.semaphore(tag + name)))
        return made[-1]

    def clear():
        engines = (nc.gpsimd, nc.sync, nc.scalar, nc.vector, nc.tensor)
        for n, s in enumerate(made):
            engines[n % len(engines)].sem_clear(s)
        nc.all_engine_barrier()

    ctx.callback(clear)
    return sem


def product3(pe, out, w_hi, w_lo, x_hi, x_lo, first, last):
    pe.matmul(out, w_hi, x_hi, start=first, stop=False)
    pe.matmul(out, w_hi, x_lo, start=False, stop=False)
    return pe.matmul(out, w_lo, x_hi, start=False, stop=last)


def ffn(nc, ctx, layer, w_up, conv_w, w_down, x_hi, x_lo, acc):
    sb, ps = buffers(nc, ctx)
    n_ = f"f{layer}_"
    sem = semaphores(nc, ctx, n_)
    raw = [sb(f"{n_}raw{i}", [P, D]) for i in range(RING)]
    w_hi = [sb(f"{n_}whi{i}", [P, D], F32R) for i in range(RING)]
    w_lo = [sb(f"{n_}wlo{i}", [P, D], F32R) for i in range(RING)]
    pad = FFN_TAPS - 1
    u = [sb(f"{n_}u{i}", [P, pad + T]) for i in range(2)]
    gate = sb(f"{n_}gate", [P, T])
    hid = sb(f"{n_}hid", [P, T])
    h_hi = [sb(f"{n_}hhi{i}", [P, T], F32R) for i in range(PAIR)]
    h_lo = [sb(f"{n_}hlo{i}", [P, T], F32R) for i in range(PAIR)]
    taps = sb(f"{n_}taps", [P, UP_TILES, FFN_TAPS])
    up_ps = [ps(f"{n_}up{i}", [P, T]) for i in range(2)]
    down_ps = [ps(f"{n_}down{i}", [P, HALF]) for i in range(4)]

    s_raw = [sem(f"w_raw{i}") for i in range(RING)]
    s_hi = sem("w_high")
    s_lo = sem("w_low")
    s_up = sem("up_product_done")
    s_taps = sem("taps_loaded")
    s_zero = sem("pads_zeroed")
    s_u = sem("u_evicted")
    s_conv = sem("conv_done")
    s_silu = sem("gate_activated")
    s_h = sem("hidden_made")
    s_hhi = sem("hidden_high")
    s_hlo = sem("hidden_low")
    s_bank = sem("down_bank_full")
    s_free = sem("down_bank_free")

    def slot(c):
        return c % RING

    def turn(g, c):
        return 2 * g + c // RING

    def first_pair(g):
        return (0, 1) if isinstance(g, int) and g == 0 else (-2, -1)

    def groups(engine, body, after):
        body(0)
        with engine.Fori(1, GROUPS) as g:
            body(g)
        after(GROUPS)

    def sync(sp):
        def load(g, c, source):
            if not (isinstance(g, int) and 6 * g + c < RING):
                sp.wait_ge(s_lo, 6 * g + c - RING + 1)
            sp.dma_start(raw[slot(c)][:, :], source.rearrange("a p f -> p (a f)")) \
                .then_inc(s_raw[slot(c)], 16)

        def up(g, c, j, value):
            load(g, c, w_up[layer, bass.ds(g * PAIR + j + value * FT, 1), :, :])

        def down(g, c, j):
            load(g, c, w_down[layer, bass.ds(g * PAIR + j - PAIR, 1), :, :])

        def body(g):
            c = first_pair(g)
            up(g, c[0], 0, 0)
            up(g, c[1], 0, 1)
            if not isinstance(g, int):
                down(g, 0, 0)
                down(g, 1, 1)
            up(g, 2, 1, 0)
            up(g, 3, 1, 1)

        sp.dma_start(taps[:, :, :], conv_w[layer]).then_inc(s_taps, 16)
        groups(sp, body, lambda g: (down(g, -2, 0), down(g, -1, 1)))

    def gpsimd(pool):
        pool.memset(u[0][:, 0:pad], 0.0)
        pool.memset(u[1][:, 0:pad], 0.0)
        pool.drain().then_inc(s_zero, 1)

        def split(g, c):
            pool.wait_ge(s_hi, 6 * g + c + 1)
            k = slot(c)
            pool.tensor_tensor(w_lo[k][:, :], raw[k][:, :], w_hi[k][:, :].bitcast(F32), ALU.subtract) \
                .then_inc(s_lo, 1)

        def body(g):
            for c in ((0, 1, 2, 3) if isinstance(g, int) else (-2, -1, 0, 1, 2, 3)):
                split(g, c)

        groups(pool, body, lambda g: (split(g, -2), split(g, -1)))

    def scalar(act):
        def high(g, c):
            act.wait_ge(s_raw[slot(c)], 16 * turn(g, c) + 16)
            if isinstance(g, int):
                if c >= RING:
                    act.wait_ge(s_up, c - RING + 1)
            elif c in (3, 4):
                act.wait_ge(s_bank, 2 * NT * g)
            else:
                act.wait_ge(s_up, 4 * g + (0, 1, 2, None, None, 3)[c])
            act.activation(w_hi[slot(c)][:, :], raw[slot(c)][:, :], ACT.Copy).then_inc(s_hi, 1)

        def evict(g, k):
            act.wait_ge(s_up, 4 * g + k + 1)
            if not (isinstance(g, int) and 4 * g + k < 2):
                act.wait_ge(s_conv, 4 * g + k - 1)
            act.activation(u[k % 2][:, pad:], up_ps[k % 2][:, :], ACT.Copy).then_inc(s_u, 1)

        def silu(g, j):
            act.wait_ge(s_conv, 4 * g + 2 * j + 1)
            act.activation(gate[:, :], gate[:, :], ACT.Silu).then_inc(s_silu, 1)

        def hidden_high(g, j):
            act.wait_ge(s_h, 2 * g + j + 1)
            if j == 0 and not isinstance(g, int):
                act.wait_ge(s_bank, 2 * NT * g)
            act.activation(h_hi[j][:, :], hid[:, :], ACT.Copy).then_inc(s_hhi, 1)

        high(0, 0)
        high(0, 1)

        def body(g):
            first = isinstance(g, int)
            if not first:
                evict(g - 1, 3)
                high(g, 0)
                hidden_high(g - 1, 1)
            evict(g, 0)
            high(g, 3 if first else 1)
            silu(g, 0)
            evict(g, 1)
            if first:
                high(g, 4)
                hidden_high(g, 0)
            else:
                high(g, 2)
                high(g, 3)
                hidden_high(g, 0)
                high(g, 4)
            evict(g, 2)
            high(g, 5)
            silu(g, 1)

        high(0, 2)
        groups(act, body, lambda g: (evict(g - 1, 3), hidden_high(g - 1, 1)))

    def add_down(dve, g, start, stop):
        for b in range(start, stop):
            dve.wait_ge(s_bank, 2 * NT * g + b + 1)
            part = acc[:, b // 2, (b % 2) * HALF:(b % 2 + 1) * HALF]
            dve.tensor_tensor(part, down_ps[b % 4][:, :], part, ALU.add).then_inc(s_free, 1)

    def add_tile(dve, c, s):
        for half in range(2):
            dve.wait_ge(s_bank, 2 * NT * (GROUPS - 1) + 2 * c + half + 1)
            part = acc[:, bass.ds(c, 1), half * HALF:(half + 1) * HALF].rearrange("p a d -> p (a d)")
            dve.tensor_tensor(part, down_ps[2 * s + half][:, :], part, ALU.add).then_inc(s_free, 1)

    def vector(dve):
        def conv(g, k, out, down=None):
            dve.wait_ge(s_u, 4 * g + k + 1)
            w = taps[:, bass.ds(g * PAIR + k // 2 + (k % 2) * FT, 1), :]
            src = u[k % 2]
            dve.tensor_scalar(out[:, :], src[:, 2:2 + T], w[:, 0, 2:3], None, ALU.mult)
            if down is not None:
                add_down(dve, down, 0, 1)
            dve.drain()
            dve.scalar_tensor_tensor(out=out[:, :], in0=src[:, 1:1 + T], scalar=w[:, 0, 1:2],
                                     in1=out[:, :], op0=ALU.mult, op1=ALU.add)
            if down is not None:
                add_down(dve, down, 1, 2)
            dve.drain()
            dve.scalar_tensor_tensor(out=out[:, :], in0=src[:, 0:T], scalar=w[:, 0, 0:1],
                                     in1=out[:, :], op0=ALU.mult, op1=ALU.add).then_inc(s_conv, 1)

        def hidden(g, j, down=None):
            conv(g, 2 * j + 1, hid, down)
            if down is not None:
                add_down(dve, down, 2, 3)
            dve.drain()
            dve.wait_ge(s_silu, 2 * g + j + 1)
            dve.tensor_tensor(hid[:, :], hid[:, :], gate[:, :], ALU.mult).then_inc(s_h, 1)

        def hidden_low(g, j):
            dve.drain()
            dve.wait_ge(s_hhi, 2 * g + j + 1)
            dve.tensor_tensor(h_lo[j][:, :], hid[:, :], h_hi[j][:, :].bitcast(F32), ALU.subtract) \
                .then_inc(s_hlo, 1)
            dve.drain()

        dve.memset(acc[:, :, :], 0.0)
        dve.wait_ge(s_taps, 16)
        dve.wait_ge(s_zero, 1)
        dve.drain().then_inc(s_free, 4)

        def body(g):
            if not isinstance(g, int):
                hidden(g - 1, 1)
                hidden_low(g - 1, 1)
            conv(g, 0, gate)
            if isinstance(g, int):
                hidden(g, 0)
            else:
                hidden(g, 0, down=g - 1)
                add_down(dve, g - 1, 3, 2 * NT)
            hidden_low(g, 0)
            conv(g, 2, gate)

        groups(dve, body, lambda g: (hidden(g - 1, 1), hidden_low(g - 1, 1)))

    def down_bank(pe, g, c, b):
        pe.wait_ge(s_free, 2 * NT * g + b + 1)
        rows = slice(b // 2 * P, (b // 2 + 1) * P)
        cols = slice((b % 2) * HALF, (b % 2 + 1) * HALF)
        for j in range(PAIR):
            s = slot(c + j)
            last = product3(pe, down_ps[b % 4][:, :], h_hi[j][:, rows], h_lo[j][:, rows],
                            w_hi[s][:, cols], w_lo[s][:, cols], j == 0, j == PAIR - 1)
        last.then_inc(s_bank, 1)

    def down_tile(pe, c):
        for b in (2 * c, 2 * c + 1):
            down_bank(pe, GROUPS - 1, -2, b)

    def tensor(pe):
        def up(g, c, k):
            pe.wait_ge(s_lo, 6 * g + c + 1)
            if not (isinstance(g, int) and 4 * g + k < 2):
                pe.wait_ge(s_u, 4 * g + k - 1)
            s = slot(c)
            for half in range(2):
                cols = slice(half * HALF, (half + 1) * HALF)
                for kt in range(KT):
                    f = slice(kt * P, (kt + 1) * P)
                    last = product3(pe, up_ps[k % 2][:, cols], w_hi[s][:, f], w_lo[s][:, f],
                                    x_hi[:, kt, cols], x_lo[:, kt, cols], kt == 0, kt == KT - 1)
            last.then_inc(s_up, 1)

        def down_ready(g, c):
            pe.wait_ge(s_lo, 6 * g + 6 + c + 2)
            pe.wait_ge(s_hlo, 2 * g + 2)

        def body(g):
            c = first_pair(g)
            up(g, c[0], 0)
            up(g, c[1], 1)
            if not isinstance(g, int):
                down_ready(g - 1, 0)
                for b in range(2 * NT):
                    down_bank(pe, g - 1, 0, b)
            up(g, 2, 2)
            up(g, 3, 3)

        groups(pe, body, lambda g: down_ready(g - 1, -2))

    return dict(sync=sync, gpsimd=gpsimd, scalar=scalar, vector=vector, tensor=tensor, down_tile=down_tile,
                add_tile=add_tile, added=s_free, added_before=4 + 2 * NT * (GROUPS - 1),
                turned=[p[:, :].rearrange("p (k t) -> p k t", k=KT) for p in up_ps], squares=gate)


def token_pass(nc, tag, consts, x_in, x_out, post_gain, pre_gain, x_hi, x_lo, acc=None, lead=None,
               mixed=None, w_out=None):
    ident, eps = consts["ident"], consts["eps"]
    ctx = ExitStack()
    with ctx:
        sb, ps = buffers(nc, ctx)
        n_ = tag + "_"
        sem = semaphores(nc, ctx, n_)

        def ring(name, shape, dt=F32, n=2):
            return [sb(f"{n_}{name}{i}", shape, dt) for i in range(n)]

        xt, xn, xs = (ring(x, [P, D]) for x in ("xt", "xn", "xs"))
        ss, std, rms = (ring(x, [P, 2]) for x in ("ss", "std", "rms"))
        post = sb(n_ + "post", [P, D])
        pre = sb(n_ + "pre", [P, D])
        turned = lead["turned"] if lead else [ps(f"{n_}turned{i}", [P, KT, P]) for i in range(2)]
        s_gain = sem("gains_loaded")
        s_xin = [sem(f"x_arrived{i}") for i in range(2)]
        s_xout = [sem(f"x_stored{i}") for i in range(2)]
        s_mstd = sem("m_deviation")
        s_post = sem("m_normed")
        s_xn = sem("x_updated")
        s_xstd = sem("x_deviation")
        s_xs = sem("x_normed")
        s_turn = sem("x_turned")
        s_xhi = sem("x_high")
        s_free = sem("turned_free")
        if w_out is not None:
            w_raw = ring("wraw", [P, D], n=4)
            w_hi = sb(n_ + "whi", [P, KT, D], F32R)
            w_lo = sb(n_ + "wlo", [P, KT, D], F32R)
            o_raw = ring("oraw", [P, KT, P])
            o_hi = ring("ohi", [P, KT, P], F32R)
            o_lo = ring("olo", [P, KT, P], F32R)
            m_ps = [ps(f"{n_}m{i}", [P, D]) for i in range(2)]
            s_wraw = [sem(f"w_raw{i}") for i in range(4)]
            s_whi = sem("w_high")
            s_wlo = [sem("w_low_even"), sem("w_low_odd")]
            s_oraw = [sem(f"mixed_arrived{i}") for i in range(2)]
            s_ohi, s_olo = sem("mixed_high"), sem("mixed_low")
            s_m = sem("m_product_done")
            squares = w_raw[0]
        elif lead:
            squares = lead["squares"]
        else:
            squares = sb(n_ + "squares", [P, D])

        def m_of(c, s):
            if w_out is not None:
                return m_ps[s][:, :]
            return acc[:, bass.ds(c, 1), :].rearrange("p a d -> p (a d)")

        updated = xn if post_gain is not None else xt
        block = ctx.enter_context(nc.Block())

        def steps(engine, step, unrolled=False):
            step(0, 0, (0,))
            step(0, 1, (0, 1))
            if unrolled:
                for c in range(2, NT - 2):
                    step(c // 2, c % 2, (0, 1, 2))
            else:
                with engine.Fori(1, NT // 2 - 1) as i:
                    step(i, 0, (0, 1, 2))
                    step(i, 1, (0, 1, 2))
            step(NT // 2 - 1, 0, (0, 1, 2))
            step(NT // 2 - 1, 1, (0, 1, 2))
            step(NT // 2, 0, (1, 2))
            step(NT // 2, 1, (2,))

        def first(i):
            return isinstance(i, int) and i == 0

        def ahead(i, s):
            return not isinstance(i, int) or 2 <= 2 * i + s < NT - 1

        @block.sync
        def _(sp):
            def load_x(c, s):
                sp.dma_start(xt[s][:, :], x_in[bass.ds(c, 1), :, :].rearrange("a p d -> p (a d)")) \
                    .then_inc(s_xin[s], 16)

            def load_mixed(c, s):
                sp.dma_start(o_raw[s][:, :, :], mixed[:, :, bass.ds(c * P, P)].rearrange("k p t -> p k t")) \
                    .then_inc(s_oraw[s], 16)

            def store(c, s):
                if x_out is not None:
                    sp.wait_ge(s_xn, c + 1)
                    sp.dma_start(x_out[bass.ds(c, 1), :, :].rearrange("a p d -> p (a d)"), xn[s][:, :]) \
                        .then_inc(s_xout[s], 16)
                else:
                    sp.wait_ge(s_xs, c + 1)

            if lead:
                lead["sync"](sp)
            if w_out is not None:
                load_mixed(0, 0)
                sp.dma_start(w_raw[0][:, :], w_out[0]).then_inc(s_wraw[0], 16)
                load_mixed(1, 1)
                for kt in range(1, KT):
                    if kt >= 4:
                        sp.wait_ge(s_wlo[kt % 2], kt // 2 - 1)
                    sp.dma_start(w_raw[kt % 4][:, :], w_out[kt]).then_inc(s_wraw[kt % 4], 16)
            load_x(0, 0)
            if post_gain is not None:
                sp.dma_start(post[:, :], post_gain.partition_broadcast(P)).then_inc(s_gain, 16)
            load_x(1, 1)
            if pre_gain is not None:
                sp.dma_start(pre[:, :], pre_gain.partition_broadcast(P)).then_inc(s_gain, 16)
            with sp.Fori(1, NT // 2) as i:
                for s in range(2):
                    if w_out is not None:
                        sp.wait_ge(s_olo, i * 2 + s - 1)
                        load_mixed(i * 2 + s, s)
                    store(i * 2 + s - 2, s)
                    load_x(i * 2 + s, s)
            for s in range(2):
                store(NT - 2 + s, s)
            if x_out is not None:
                for s in range(2):
                    sp.wait_ge(s_xout[s], 16 * (NT // 2))

        @block.scalar
        def _(act):
            def mixed_high(i, s):
                act.wait_ge(s_oraw[s], 16 * i + 16)
                if not first(i):
                    act.wait_ge(s_m, i * 2 + s - 1)
                act.activation(o_hi[s][:, :, :], o_raw[s][:, :, :], ACT.Copy).then_inc(s_ohi, 1)

            def m_deviation(i, s):
                if w_out is not None:
                    act.wait_ge(s_m, i * 2 + s + 1)
                if lead:
                    act.wait_ge(lead["added"], lead["added_before"] + 2 * (i * 2 + s + 1))
                if not first(i):
                    act.wait_ge(s_post, i * 2 + s - 1)
                act.activation(squares[:, :], m_of(i * 2 + s, s), ACT.Square, accum_out=ss[s][:, 0:1])
                act.drain()
                act.activation(std[s][:, 0:1], ss[s][:, 0:1], ACT.Sqrt, scale=1.0 / D,
                               bias=eps[:, 0:1]).then_inc(s_mstd, 1)

            def x_deviation(i, s):
                if post_gain is not None:
                    act.wait_ge(s_xn, i * 2 + s)
                else:
                    act.wait_ge(s_xin[1 - s], 16 * (i + s))
                act.activation(squares[:, :], updated[1 - s][:, :], ACT.Square, accum_out=ss[1 - s][:, 1:2])
                act.drain()
                act.activation(std[1 - s][:, 1:2], ss[1 - s][:, 1:2], ACT.Sqrt, scale=1.0 / D,
                               bias=eps[:, 0:1]).then_inc(s_xstd, 1)

            if lead:
                lead["scalar"](act)
            if w_out is not None:
                mixed_high(0, 0)
                for kt in range(KT):
                    act.wait_ge(s_wraw[kt % 4], 16 * (kt // 4 + 1))
                    act.activation(w_hi[:, kt, :], w_raw[kt % 4][:, :], ACT.Copy).then_inc(s_whi, 1)
                    if kt == 0:
                        mixed_high(0, 1)

            def step(i, s, lags):
                if w_out is not None and first(i) and s == 0:
                    mixed_high(1, 0)
                elif w_out is not None and ahead(i, s):
                    mixed_high(i + s, 1 - s)
                if post_gain is not None and 0 in lags:
                    m_deviation(i, s)
                if pre_gain is None:
                    return
                if 1 in lags:
                    x_deviation(i, s)
                if 2 in lags:
                    act.wait_ge(s_turn, i * 2 + s - 1)
                    act.activation(x_hi[:, :, bass.ds((i * 2 + s - 2) * P, P)], turned[s][:, :, :], ACT.Copy) \
                        .then_inc(s_xhi, 1)

            steps(act, step)

        def split_weight(engine, kt):
            engine.wait_ge(s_whi, kt + 1)
            engine.tensor_tensor(w_lo[:, kt, :], w_raw[kt % 4][:, :], w_hi[:, kt, :].bitcast(F32),
                                 ALU.subtract).then_inc(s_wlo[kt % 2], 1)

        def mixed_low(engine, i, s):
            engine.wait_ge(s_ohi, i * 2 + s + 1)
            engine.tensor_tensor(o_lo[s][:, :, :], o_raw[s][:, :, :], o_hi[s][:, :, :].bitcast(F32),
                                 ALU.subtract).then_inc(s_olo, 1)

        @block.gpsimd
        def _(pool):
            def step(i, s, lags):
                if w_out is not None and first(i) and s == 0:
                    mixed_low(pool, 1, 0)
                elif w_out is not None and ahead(i, s):
                    mixed_low(pool, i + s, 1 - s)
                if post_gain is not None and 0 in lags:
                    pool.wait_ge(s_post, i * 2 + s + 1)
                    pool.wait_ge(s_xin[s], 16 * i + 16)
                    pool.tensor_tensor(xn[s][:, :], xn[s][:, :], xt[s][:, :], ALU.add).then_inc(s_xn, 1)

            if lead:
                lead["gpsimd"](pool)
            if w_out is not None:
                for kt in range(0, KT, 2):
                    split_weight(pool, kt)
            steps(pool, step)

        @block.vector
        def _(dve):
            def step(i, s, lags):
                if lead and 0 in lags and not (isinstance(i, int) and 2 * i + s >= NT - 1):
                    lead["add_tile"](dve, i * 2 + s + 1, 1 - s)
                if post_gain is not None and 0 in lags:
                    dve.wait_ge(s_mstd, i * 2 + s + 1)
                    dve.reciprocal(rms[s][:, 0:1], std[s][:, 0:1])
                    dve.drain()
                    if x_out is not None and not first(i):
                        dve.wait_ge(s_xout[s], 16 * i)
                    dve.scalar_tensor_tensor(out=xn[s][:, :], in0=m_of(i * 2 + s, s), scalar=rms[s][:, 0:1],
                                             in1=post[:, :], op0=ALU.mult, op1=ALU.mult).then_inc(s_post, 1)
                if pre_gain is None:
                    return
                if 1 in lags:
                    b = 1 - s
                    dve.wait_ge(s_xstd, i * 2 + s)
                    dve.reciprocal(rms[b][:, 1:2], std[b][:, 1:2])
                    dve.drain()
                    dve.scalar_tensor_tensor(out=xs[b][:, :], in0=updated[b][:, :], scalar=rms[b][:, 1:2],
                                             in1=pre[:, :], op0=ALU.mult, op1=ALU.mult).then_inc(s_xs, 1)
                if 2 in lags:
                    at = bass.ds((i * 2 + s - 2) * P, P)
                    dve.wait_ge(s_xhi, i * 2 + s - 1)
                    dve.tensor_tensor(x_lo[:, :, at], turned[s][:, :, :], x_hi[:, :, at].bitcast(F32),
                                      ALU.subtract).then_inc(s_free, 1)

            if lead:
                lead["vector"](dve)
                lead["add_tile"](dve, 0, 0)
            if w_out is not None:
                mixed_low(dve, 0, 0)
                mixed_low(dve, 0, 1)
                for kt in range(1, KT, 2):
                    split_weight(dve, kt)
            dve.wait_ge(s_gain, 16 * ((post_gain is not None) + (pre_gain is not None)))
            dve.drain().then_inc(s_free, 2)
            steps(dve, step)

        @block.tensor
        def _(pe):
            def weights_arrive():
                for kt in range(KT):
                    pe.wait_ge(s_wlo[kt % 2], kt // 2 + 1)
                    for s in range(2):
                        if kt == 0:
                            pe.wait_ge(s_olo, s + 1)
                        for half in range(2):
                            last = product(s, half, kt)
                        if kt == KT - 1:
                            last.then_inc(s_m, 1)

            def product(s, half, kt):
                cols = slice(half * HALF, (half + 1) * HALF)
                return product3(pe, m_ps[s][:, cols], o_hi[s][:, kt, :], o_lo[s][:, kt, :], w_hi[:, kt, cols],
                                w_lo[:, kt, cols], kt == 0, kt == KT - 1)

            def step(i, s, lags):
                if w_out is not None and 0 in lags and not first(i):
                    pe.wait_ge(s_olo, i * 2 + s + 1)
                    pe.wait_ge(s_post, i * 2 + s - 1)
                    for half in range(2):
                        for kt in range(KT):
                            last = product(s, half, kt)
                    last.then_inc(s_m, 1)
                if lead and 0 in lags and 2 * i + s + 2 < NT:
                    lead["down_tile"](pe, 2 * i + s + 2)
                if pre_gain is not None and 2 in lags:
                    pe.wait_ge(s_xs, i * 2 + s - 1)
                    pe.wait_ge(s_free, i * 2 + s - 1)
                    for kt in range(KT):
                        last = pe.transpose(turned[s][:, kt, :], xs[s][:, kt * P:(kt + 1) * P], ident[:, :])
                    last.then_inc(s_turn, 1)

            if lead:
                lead["tensor"](pe)
                lead["down_tile"](pe, 0)
                lead["down_tile"](pe, 1)
            if w_out is not None:
                weights_arrive()
            steps(pe, step, unrolled=bool(lead))


def constants(nc, ctx):
    sb, _ = buffers(nc, ctx)
    ident = sb("ident", [P, P])
    upper = sb("upper", [P, P])
    ones = sb("ones", [P, P])
    eps = sb("eps", [P, 1])
    sizes = tuple(2 ** n for n in range(7))
    masks = sb("masks", [P, len(sizes), P])
    with nc.Block() as block:
        @block.gpsimd
        def _(pool):
            for n, s in enumerate(sizes):
                pool.memset(masks[:, n, :], 1.0)
            pool.drain()
            for n, s in enumerate(sizes):
                blocks = P // (2 * s)
                m = masks[:, n, :].rearrange("p (b half t) -> p b half t", half=2, t=s)
                pool.memset(m[:, :, 0, :], 0.0)
                for pattern, base, mult in (([[-2 * s, blocks], [0, s]], 0, 1),
                                            ([[2 * s, blocks], [0, s]], s - 1, -1)):
                    pool.drain()
                    pool.affine_select(out=m[:, :, 1, :], in_=m[:, :, 1, :], compare_op=ALU.is_ge, fill=0.0,
                                       base=base, pattern=pattern, channel_multiplier=mult)
            pool.memset(ident[:, :], 0.0)
            pool.memset(upper[:, :], 1.0)
            pool.memset(ones[:, :], 1.0)
            pool.memset(eps[:, :], EPS)
            pool.drain()
            pool.affine_select(out=ident[:, :], in_=ident[:, :], compare_op=ALU.not_equal, fill=1.0, base=0,
                               pattern=[[-1, P]], channel_multiplier=1)
            pool.affine_select(out=upper[:, :], in_=upper[:, :], compare_op=ALU.is_ge, fill=0.0, base=0,
                               pattern=[[1, P]], channel_multiplier=-1)
    return dict(ident=ident, upper=upper, ones=ones, eps=eps, masks=masks)


GDN_HEADS = 8
GDN_TAPS = 4
GATE_KINDS = 6
G_LOG, G_BETA, G_CUM, G_CUM_EXP, G_TO_END, G_CHUNK = range(GATE_KINDS)
LEVELS = (2, 4, 8, 16, 32, 64)
SLOTS = 2


def token_logits(pe, out, x_hi, x_lo, w_hi, w_lo):
    for half in range(2):
        t = slice(half * HALF, (half + 1) * HALF)
        for kt in range(KT):
            last = product3(pe, out[:, t], w_hi[:, kt, :], w_lo[:, kt, :], x_hi[:, kt, t], x_lo[:, kt, t],
                            kt == 0, kt == KT - 1)
    return last


def wide(column, n=P):
    return column.unsqueeze(2).to_broadcast([P, column.shape[1], n])


def each(mask, n=NT):
    return mask.unsqueeze(1).to_broadcast([P, n, mask.shape[1]])


def gdn(nc, consts, w_in, w_gates, conv_w, a_log, dt_bias, o_gain, x_hi, x_lo, mixed):
    ident, upper, eps = consts["ident"], consts["upper"], consts["eps"]
    ctx = ExitStack()
    with ctx:
        sb, ps = buffers(nc, ctx)
        sem = semaphores(nc, ctx, "g_")
        H = GDN_HEADS
        raw = [sb(f"g_raw{i}", [P, D]) for i in range(SLOTS)]
        w_hi = [sb(f"g_whi{i}", [P, D], F32R) for i in range(SLOTS)]
        w_lo = [sb(f"g_wlo{i}", [P, D], F32R) for i in range(SLOTS)]
        pad = GDN_TAPS - 1
        u = [sb(f"g_u{i}", [P, pad + T]) for i in range(2)]
        taps = sb("g_taps", [P, 3 * H, GDN_TAPS])
        qkv = [sb(f"g_{x}T", [P, T]) for x in "qkv"]
        z = sb("g_z", [P, T])

        def chunks(name):
            return sb("g_" + name, [P, NT, P])

        kn = chunks("kn")
        kb = chunks("kb")
        vb = chunks("vb")
        decay = chunks("decay")
        attn = chunks("attn")
        aT = chunks("aT")
        inv = chunks("inv")
        invT = chunks("invT")
        cT = [chunks(f"cT{i}") for i in range(2)]
        from_start = cT[1]
        m1 = chunks("m1")
        wTn = chunks("wTn")
        qdT = chunks("qdT")
        zc = sb("g_zc", [P, T])
        on = chunks("on")
        og = sb("g_og", [P, T])
        vn = [sb(f"g_vn{i}", [P, P]) for i in range(2)]
        state = sb("g_state", [P, P])
        gates = sb("g_gates", [P, H, GATE_KINDS, NT])
        hg = sb("g_hg", [P, GATE_KINDS, NT])
        gate_raw = sb("g_gateraw", [P, KT, 2 * H])
        gate_hi = sb("g_gatehi", [P, KT, 2 * H], F32R)
        gate_lo = sb("g_gatelo", [P, KT, 2 * H], F32R)
        rate = sb("g_rate", [P, H])
        dt = sb("g_dt", [P, H])
        g_y, g_abs, g_den, g_log = (sb(f"g_gate{x}", [P, H, NT]) for x in ("y", "abs", "den", "log"))
        logitsT = m1[0:2 * H, :, :].rearrange("p c t -> p (c t)")
        chunk_decay = sb("g_cd", [P, NT])
        gain = sb("g_gain", [P, 1])
        std, rs = (sb(f"g_{x}", [P, 2 * NT]) for x in ("std", "rs"))
        factor = sb("g_factor", [P, NT])
        factor_end = sb("g_factorend", [P, NT])
        rq = sb("g_rq", [P, NT])
        sso, stdo, rso = (sb(f"g_{x}", [P, NT]) for x in ("sso", "stdo", "rso"))
        masks = consts["masks"]

        pa = ps("g_pa", [P, T])
        pm = ps("g_pm", [P, T])
        pt = ps("g_pt", [P, 2 * T])

        logitsT_ps = pt[0:2 * H, 0:T]
        logits_ps = pt[:, T:T + NT * 2 * H].rearrange("p (c n) -> p c n", c=NT)
        b_logits = logits_ps[:, :, 0:H].rearrange("p c h -> p h c")
        a_logits = logits_ps[:, :, H:2 * H].rearrange("p c h -> p h c")
        cum_ps, total_ps = (pt[:, T + HALF + i * H * NT:T + HALF + (i + 1) * H * NT] for i in range(2))

        norms_ps = pt[:, T:T + 2 * NT]

        def by_chunk(psum, at=0):
            return psum[:, at:at + T].rearrange("p (c t) -> p c t", c=NT)

        s_raw = [sem(f"w_raw{i}") for i in range(SLOTS)]
        s_hi, s_lo = sem("w_high"), sem("w_low")
        s_gw, s_gwhi, s_gwlo = sem("gate_w_raw"), sem("gate_w_high"), sem("gate_w_low")
        s_rates = sem("rates_loaded")
        s_lp, s_lc, s_lt = sem("gate_logits_in_psum"), sem("gate_logits_copied"), sem("gate_logits_turned")
        s_gy, s_gx, s_gl = sem("gate_input_made"), sem("gate_exps_made"), sem("log_decay_made")
        s_gc, s_gr, s_gates = sem("decay_summed"), sem("decay_relative"), sem("gates_made")
        s_taps = sem("taps_loaded")
        s_set = sem("pads_set")
        s_a = sem("projection_half_done")
        s_u = sem("projection_half_evicted")
        s_conv, s_silu = sem("conv_done"), sem("conv_activated")
        s_tok = sem("token_major_in_psum")
        s_sq, s_ss, s_std = sem("squares_made"), sem("squares_summed"), sem("norms_made")
        s_fac = sem("key_factors_made")
        s_kc, s_vb = sem("keys_copied"), sem("values_scaled")
        s_gb, s_gcb = sem("log_decay_repeated"), sem("decay_by_columns_in_psum")
        s_dm, s_dx = sem("decay_exponent_made"), sem("decay_exps_made")
        s_g = sem("chunk_products_done")
        s_at = sem("coupling_matrix_made")
        s_ap = sem("chunk_products_decayed")
        s_pair, s_pairT, s_invc = sem("pairs_inverted"), sem("pairs_turned"), sem("pairs_copied")
        s_ct, s_m1p, s_m1 = sem("coupling_made"), sem("coupling_product_done"), sem("coupling_product_copied")
        s_x, s_t = sem("join_products_done"), sem("blocks_joined")
        s_kx = sem("keys_decayed")
        s_qd = sem("queries_decayed")
        s_w, s_wn = sem("w_product_done"), sem("w_copied")
        s_zc = sem("z_activated")
        s_vnp, s_vn = sem("new_value_done"), sem("new_value_copied")
        s_kdp, s_state = sem("chunk_output_done"), sem("state_updated")
        s_sqo, s_sso, s_stdo = sem("output_squares_made"), sem("output_squares_summed"), sem("output_deviation")
        s_on, s_oT, s_og, s_ost = sem("output_normed"), sem("output_turned"), sem("output_gated"), sem("output_stored")
        L = 2 * len(LEVELS)

        def peeled(h):
            return isinstance(h, int) and h == 0

        block = ctx.enter_context(nc.Block())

        def final(h):
            return isinstance(h, int) and h == H - 1

        def heads(engine, body, after):
            body(0)
            with engine.Fori(1, H - 1) as h:
                body(h)
            body(H - 1)
            after(H)

        @block.sync
        def _(sp):
            sp.dma_start(gate_raw[:, :, :], w_gates).then_inc(s_gw, 16)

            def load(n, k):
                sp.dma_start(raw[k % SLOTS][:, :], w_in[bass.ds(n, 1), :, :].rearrange("a p f -> p (a f)")) \
                    .then_inc(s_raw[k % SLOTS], 16)

            def store(h):
                sp.wait_ge(s_og, h + 1)
                sp.dma_start(mixed[bass.ds(h, 1), :, :].rearrange("a p t -> p (a t)"), og[:, :]) \
                    .then_inc(s_ost, 16)

            load(0, 0)
            load(1, 1)
            sp.dma_start(rate[:, :], a_log.partition_broadcast(P)).then_inc(s_rates, 16)
            sp.dma_start(dt[:, :], dt_bias.partition_broadcast(P)).then_inc(s_rates, 16)
            sp.dma_start(taps[:, :, :], conv_w).then_inc(s_taps, 16)
            sp.dma_start(gain[:, :], o_gain).then_inc(s_taps, 16)

            def body(h):
                for k in range(SLOTS, 4 if final(h) else 4 + SLOTS):
                    sp.wait_ge(s_lo, 4 * h + k - SLOTS + 1)
                    load(4 * h + k, k)
                if not peeled(h):
                    store(h - 1)

            heads(sp, body, lambda h: store(h - 1))
            sp.wait_ge(s_ost, 16 * H)

        @block.gpsimd
        def _(pool):
            for i in range(2):
                pool.memset(u[i][:, 0:pad], 0.0)
            pool.drain().then_inc(s_set, 1)

            def split(h, k):
                pool.wait_ge(s_hi, 4 * h + k + 1)
                s = k % SLOTS
                pool.tensor_tensor(w_lo[s][:, :], raw[s][:, :], w_hi[s][:, :].bitcast(F32), ALU.subtract) \
                    .then_inc(s_lo, 1)

            def coupling(h, n):
                if n == 0:
                    pool.wait_ge(s_at, h + 1)
                elif n == 1:
                    pool.wait_ge(s_qd, h + 1)
                else:
                    pool.wait_ge(s_m1p, L * h + 2 * (n - 1))
                pool.tensor_tensor(cT[n % 2][:, :, :], aT[:, :, :], each(masks[:, n + 1, :]), ALU.mult) \
                    .then_inc(s_ct, 1)

            split(0, 0)
            split(0, 1)

            def body(h):
                split(h, 2)
                split(h, 3)
                if not final(h):
                    split(h, 4)
                pool.wait_ge(s_kc, h + 1)
                pool.tensor_tensor(kb[:, :, :], kn[:, :, :], wide(hg[:, G_CUM_EXP, :]), ALU.mult).then_inc(s_kx, 1)
                pool.drain()
                pool.wait_ge(s_fac, h + 1)
                pool.tensor_tensor(kn[:, :, :], kn[:, :, :], wide(factor_end[:, :]), ALU.mult).then_inc(s_kx, 1)
                coupling(h, 0)
                coupling(h, 1)
                if not final(h):
                    split(h, 5)
                for n in range(2, len(LEVELS)):
                    coupling(h, n)

            heads(pool, body, lambda h: None)

        @block.scalar
        def _(act):
            def high(h, k):
                act.wait_ge(s_raw[k % SLOTS], 16 * (2 * h + k // 2) + 16)
                if not (peeled(h) and k < SLOTS):
                    act.wait_ge(s_a, 8 * h + 2 * (k - SLOTS) + 2)
                act.activation(w_hi[k % SLOTS][:, :], raw[k % SLOTS][:, :], ACT.Copy).then_inc(s_hi, 1)

            def evict(h, *halves):
                for j in halves:
                    k, half = j // 2, j % 2
                    act.wait_ge(s_a, 8 * h + j + 1)
                    cols = slice(half * HALF, (half + 1) * HALF)
                    out = z[:, cols] if k == 3 else u[k % 2][:, pad + half * HALF:pad + (half + 1) * HALF]
                    act.activation(out, pa[:, cols], ACT.Copy).then_inc(s_u, 1)

            def silu(h, k):
                act.wait_ge(s_conv, 3 * h + k + 1)
                act.activation(qkv[k][:, :], qkv[k][:, :], ACT.Silu).then_inc(s_silu, 1)

            def project(h):
                high(h, 2)
                act.wait_ge(s_dm, h + 1)
                act.activation(decay[:, :, :], decay[:, :, :], ACT.Exp).then_inc(s_dx, 1)
                act.activation(from_start[:, :, :], by_chunk(pm), ACT.Exp).then_inc(s_dx, 1)
                silu(h, 0)
                act.drain()
                act.activation(inv[:, :, :], by_chunk(qkv[0]), ACT.Square).then_inc(s_sq, 1)
                evict(h, 2, 3)
                high(h, 3)
                evict(h, 4, 5)
                if not final(h):
                    high(h, 4)
                silu(h, 1)
                act.drain()
                act.activation(aT[:, :, :], by_chunk(qkv[1]), ACT.Square).then_inc(s_sq, 1)

            def output_squares(h):
                act.wait_ge(s_kdp, 8 * h + 8)
                act.activation(on[:, :, :], by_chunk(pt), ACT.Square).then_inc(s_sqo, 1)

            def output_deviation(h):
                act.wait_ge(s_sso, h + 1)
                act.activation(stdo[:, :], sso[:, :], ACT.Sqrt, scale=1.0 / P, bias=eps[:, 0:1]) \
                    .then_inc(s_stdo, 1)

            def prepare(h):
                if not peeled(h):
                    output_squares(h - 1)
                act.wait_ge(s_ss, h + 1)
                act.activation(std[:, :], norms_ps, ACT.Sqrt, bias=eps[:, 0:1]).then_inc(s_std, 1)
                act.wait_ge(s_tok, 2 * h + 1)
                act.activation(kn[:, :, :], by_chunk(pm), ACT.Copy).then_inc(s_kc, 1)
                if not peeled(h):
                    output_deviation(h - 1)
                silu(h, 2)
                evict(h, 6)
                evict(h, 7)
                if not final(h):
                    high(h, 5)
                    evict(h, 8)
                act.wait_ge(s_pairT, h + 1)
                act.activation(inv[:, :, :], by_chunk(pm), ACT.Copy).then_inc(s_invc, 1)
                for n in range(L):
                    part = slice(n % 2 * 4, n % 2 * 4 + 4)
                    act.wait_ge(s_m1p, L * h + n + 1)
                    if n < L - 2:
                        out, psum = m1[:, part, :], by_chunk(pm)[:, part, :]
                    else:
                        out, psum = m1[:, part, 0:P // 2], by_chunk(pm)[:, part, 0:P // 2]
                    act.activation(out, psum, ACT.Copy).then_inc(s_m1, 1)
                act.wait_ge(s_w, h + 1)
                act.activation(wTn[:, :, :], by_chunk(pm), ACT.Copy, scale=-1.0).then_inc(s_wn, 1)
                if not final(h):
                    evict(h, 9)
                if not peeled(h):
                    act.wait_ge(s_og, h)
                act.activation(zc[:, :], z[:, :], ACT.Silu).then_inc(s_zc, 1)

            def gate_exps():
                act.wait_ge(s_rates, 32)
                act.activation(rate[:, :], rate[:, :], ACT.Exp)
                act.wait_ge(s_gy, 1)
                act.activation(g_den[:, :, :], g_den[:, :, :], ACT.Exp)
                act.activation(g_abs[:, :, :], g_abs[:, :, :], ACT.Exp, scale=-1.0)
                act.drain()
                act.activation(g_abs[:, :, :], g_abs[:, :, :], ACT.Ln, bias=consts["ones"][:, 0:1]).then_inc(s_gx, 1)
                act.wait_ge(s_gr, 1)
                act.activation(gates[:, :, G_CUM_EXP, :], gates[:, :, G_CUM, :], ACT.Exp)
                act.activation(gates[:, :, G_TO_END, :], g_abs[:, :, :], ACT.Exp)
                act.activation(gates[:, :, G_CHUNK, :], total_ps.rearrange("p (h c) -> p h c", h=H), ACT.Exp)
                act.drain().then_inc(s_gates, 1)

            act.wait_ge(s_gw, 16)
            act.activation(gate_hi[:, :, :], gate_raw[:, :, :], ACT.Copy).then_inc(s_gwhi, 1)
            high(0, 0)
            high(0, 1)
            gate_exps()
            evict(0, 0, 1)

            def body(h):
                project(h)
                prepare(h)

            heads(act, body, lambda h: (output_squares(h - 1), output_deviation(h - 1)))

        @block.vector
        def _(dve):
            def conv_taps(h, k, some):
                x, src = qkv[k], u[k % 2]
                w = taps[:, bass.ds(3 * h + k, 1), :]
                for n in some:
                    tap = pad - n
                    dve.drain()
                    if n == 0:
                        dve.wait_ge(s_u, 8 * h + 2 * k + 2)
                        dve.tensor_scalar(x[:, :], src[:, tap:tap + T], w[:, 0, tap:tap + 1], None, ALU.mult)
                    else:
                        ins = dve.scalar_tensor_tensor(out=x[:, :], in0=src[:, tap:tap + T],
                                                       scalar=w[:, 0, tap:tap + 1], in1=x[:, :],
                                                       op0=ALU.mult, op1=ALU.add)
                        if n == pad:
                            ins.then_inc(s_conv, 1)

            def new_value(h, c):
                dve.wait_ge(s_vnp, 8 * h + c + 1)
                dve.tensor_copy(vn[c % 2][:, :], pt[:, T:T + P]).then_inc(s_vn, 1)

            def update_state(h, c):
                added = pt[:, T + HALF:T + HALF + P]
                dve.drain()
                dve.wait_ge(s_kdp, 8 * h + c + 1)
                if c == 0:
                    dve.tensor_copy(state[:, :], added).then_inc(s_state, 1)
                else:
                    dve.scalar_tensor_tensor(out=state[:, :], in0=state[:, :], scalar=chunk_decay[:, c:c + 1],
                                             in1=added, op0=ALU.mult, op1=ALU.add).then_inc(s_state, 1)

            def head_decay(h):
                dve.wait_ge(s_gcb, h + 1)
                dve.tensor_tensor(decay[:, :, :], by_chunk(pm), wide(hg[:, G_CUM, :]), ALU.subtract)
                dve.drain()
                dve.tensor_scalar(decay[:, :, :], decay[:, :, :], 0.0, None, ALU.min).then_inc(s_dm, 1)

            def mask_decay(h):
                dve.wait_ge(s_dx, 2 * h + 1)
                dve.tensor_tensor(decay[:, :, :], decay[:, :, :], each(upper[:, :]), ALU.mult)

            def project_and_scan(h, projects, scans):
                beside = {}
                if projects:
                    dve.drain()
                    if not peeled(h):
                        dve.wait_ge(s_kx, 2 * h)
                    dve.tensor_copy(hg[:, :, :].unsqueeze(1), gates[:, bass.ds(h, 1), :, :])
                    dve.drain()
                    dve.tensor_copy(m1[:, :, :], wide(hg[:, G_LOG, :])).then_inc(s_gb, 1)
                    beside = {0: lambda: conv_taps(h, 0, (0,)), 1: lambda: head_decay(h),
                              2: lambda: conv_taps(h, 0, (1, 2)), 3: lambda: conv_taps(h, 0, (3,)),
                              4: lambda: mask_decay(h), 5: lambda: conv_taps(h, 1, (0, 1)),
                              6: lambda: conv_taps(h, 1, (2,)), 7: lambda: conv_taps(h, 1, (3,))}
                for n in range(NT):
                    if scans:
                        new_value(h - 1, n)
                    if n in beside:
                        beside[n]()
                    if scans and n < NT - 1:
                        update_state(h - 1, n)

            def output_sums(h):
                dve.wait_ge(s_sqo, h + 1)
                dve.tensor_reduce(out=sso[:, :], in_=on[:, :, :], axis=AX_X, op=ALU.add)
                dve.drain()
                dve.tensor_tensor(sso[:, :], sso[:, :], rq[:, :], ALU.mult)
                dve.drain()
                dve.tensor_tensor(sso[:, :], sso[:, :], rq[:, :], ALU.mult).then_inc(s_sso, 1)

            def output_norm(h):
                dve.wait_ge(s_stdo, h + 1)
                dve.reciprocal(rso[:, :], stdo[:, :])
                dve.drain()
                dve.tensor_tensor(rso[:, :], rso[:, :], rq[:, :], ALU.mult)
                dve.drain()
                dve.tensor_tensor(on[:, :, :], by_chunk(pt), wide(rso[:, :]), ALU.mult).then_inc(s_on, 1)

            def output_gate(h):
                dve.wait_ge(s_zc, h + 1)
                if not (isinstance(h, int) and h == 0):
                    dve.wait_ge(s_ost, 16 * h)
                dve.wait_ge(s_oT, h + 1)
                dve.scalar_tensor_tensor(out=og[:, :], in0=pt[:, T:2 * T], scalar=gain[:, 0:1], in1=zc[:, :],
                                         op0=ALU.mult, op1=ALU.mult).then_inc(s_og, 1)

            def prepare(h):
                conv_taps(h, 2, (0, 1))
                if not peeled(h):
                    output_sums(h - 1)
                conv_taps(h, 2, (2, 3))
                dve.wait_ge(s_std, h + 1)
                dve.reciprocal(rs[:, :], std[:, :])
                dve.drain()
                dve.tensor_tensor(factor[:, :], rs[:, 0:NT], rs[:, 0:NT], ALU.mult)
                dve.drain()
                dve.tensor_tensor(factor[:, :], factor[:, :], hg[:, G_BETA, :], ALU.mult)
                dve.drain()
                dve.tensor_tensor(factor_end[:, :], factor[:, :], hg[:, G_TO_END, :], ALU.mult).then_inc(s_fac, 1)
                dve.tensor_tensor(decay[:, :, :], decay[:, :, :], wide(factor[:, :]), ALU.mult)
                if not peeled(h):
                    output_norm(h - 1)
                dve.tensor_scalar(rq[:, :], rs[:, NT:2 * NT], float(P) ** -0.5, None, ALU.mult)
                dve.tensor_copy(chunk_decay[:, :], hg[:, G_CHUNK, :])
                dve.wait_ge(s_tok, 2 * h + 2)
                dve.tensor_tensor(vb[:, :, :], by_chunk(pm), wide(std[:, 0:NT]), ALU.mult).then_inc(s_vb, 1)
                if not peeled(h):
                    output_gate(h - 1)
                dve.drain()
                dve.wait_ge(s_g, h + 1)
                products = pt[:, :].rearrange("p (c t) -> p c t", c=NT)
                dve.tensor_tensor(aT[:, :, :], products[:, :, 0:P], decay[:, :, :], ALU.mult).then_inc(s_at, 1)
                dve.drain()
                dve.tensor_tensor(invT[:, :, :], aT[:, :, :], each(masks[:, 0, :]), ALU.mult)
                dve.drain()
                dve.tensor_tensor(invT[:, :, :], each(ident[:, :]), invT[:, :, :], ALU.subtract).then_inc(s_pair, 1)
                dve.tensor_tensor(attn[:, :, :], products[:, :, P:2 * P], decay[:, :, :], ALU.mult).then_inc(s_ap, 1)
                dve.tensor_tensor(qdT[:, :, :], by_chunk(qkv[0]), from_start[:, :, :], ALU.mult).then_inc(s_qd, 1)
                for n in range(len(LEVELS)):
                    last = n == len(LEVELS) - 1
                    for a in range(2):
                        part = slice(a * 4, a * 4 + 4)
                        dve.drain()
                        if n == 0 and a == 0:
                            dve.wait_ge(s_invc, h + 1)
                        dve.wait_ge(s_x, L * h + 2 * n + a + 1)
                        x = pt[:, a * T:(a + 1) * T].rearrange("p (m c t) -> p m c t", m=2, c=4)
                        if last:
                            low, high = slice(0, P // 2), slice(P // 2, P)
                            dve.tensor_tensor(invT[low, part, high], invT[low, part, high], x[low, 1, :, high],
                                              ALU.subtract).then_inc(s_t, 1)
                            continue
                        dve.tensor_tensor(inv[:, part, :], inv[:, part, :], x[:, 0], ALU.subtract)
                        dve.tensor_tensor(invT[:, part, :], invT[:, part, :], x[:, 1], ALU.subtract) \
                            .then_inc(s_t, 1)

            def make_gates():
                dve.wait_ge(s_gwhi, 1)
                dve.tensor_tensor(gate_lo[:, :, :], gate_raw[:, :, :], gate_hi[:, :, :].bitcast(F32),
                                  ALU.subtract).then_inc(s_gwlo, 1)
                dve.wait_ge(s_lp, 1)
                dve.tensor_copy(logitsT, logitsT_ps).then_inc(s_lc, 1)
                dve.wait_ge(s_rates, 32)
                dve.wait_ge(s_lt, 1)
                dve.tensor_scalar(g_den[:, :, :], b_logits, -1.0, None, ALU.mult)
                dve.tensor_tensor(g_y[:, :, :], a_logits, dt[:, :].unsqueeze(2).to_broadcast([P, H, NT]), ALU.add)
                dve.drain()
                dve.scalar_tensor_tensor(out=g_abs[:, :, :], in0=g_y[:, :, :], scalar=-1.0, in1=g_y[:, :, :],
                                         op0=ALU.mult, op1=ALU.max).then_inc(s_gy, 1)
                dve.wait_ge(s_gx, 1)
                dve.scalar_tensor_tensor(out=g_y[:, :, :], in0=g_y[:, :, :], scalar=0.0, in1=g_abs[:, :, :],
                                         op0=ALU.max, op1=ALU.add)
                dve.tensor_scalar(g_den[:, :, :], g_den[:, :, :], 1.0, None, ALU.add)
                dve.drain()
                dve.scalar_tensor_tensor(out=g_log[:, :, :], in0=g_y[:, :, :], scalar=-1.0,
                                         in1=rate[:, :].unsqueeze(2).to_broadcast([P, H, NT]),
                                         op0=ALU.mult, op1=ALU.mult).then_inc(s_gl, 1)
                dve.drain()
                dve.tensor_copy(gates[:, :, G_LOG, :], g_log[:, :, :])
                dve.reciprocal(gates[:, :, G_BETA, :], g_den[:, :, :])
                dve.wait_ge(s_gc, 1)
                dve.tensor_copy(gates[:, :, G_CUM, :], cum_ps.rearrange("p (h c) -> p h c", h=H))
                dve.drain()
                dve.tensor_tensor(g_abs[:, :, :], total_ps.rearrange("p (h c) -> p h c", h=H),
                                  gates[:, :, G_CUM, :], ALU.subtract).then_inc(s_gr, 1)
                dve.wait_ge(s_gates, 1)

            make_gates()
            dve.wait_ge(s_taps, 32)
            dve.wait_ge(s_set, 1)

            def body(h):
                project_and_scan(h, True, not peeled(h))
                prepare(h)

            heads(dve, body, lambda h: (project_and_scan(h, False, True), output_sums(h - 1),
                                        output_norm(h - 1), output_gate(h - 1)))

        @block.tensor
        def _(pe):
            def project_parts(h, start, count):
                for n in range(start, start + count):
                    if final(h) and n >= 32:
                        return
                    k, half, part = n // 8, n // 4 % 2, n % 4
                    s = k % SLOTS
                    cols = slice(half * HALF, (half + 1) * HALF)
                    if part == 0:
                        pe.wait_ge(s_lo, 4 * h + k + 1)
                        if not (peeled(h) and n < 8):
                            pe.wait_ge(s_u, 8 * h + n // 4 - 1)
                    for kt in range(part * KT // 4, (part + 1) * KT // 4):
                        f = slice(kt * P, (kt + 1) * P)
                        last = product3(pe, pa[:, cols], w_hi[s][:, f], w_lo[s][:, f], x_hi[:, kt, cols],
                                        x_lo[:, kt, cols], kt == 0, kt == KT - 1)
                    if part == 3:
                        last.then_inc(s_a, 1)

            def scan_value(h, c):
                out = pt[:, T:T + P]
                if c == 0:
                    pe.matmul(out, invT[:, c, :], vb[:, c, :], start=True, stop=True).then_inc(s_vnp, 1)
                    return
                pe.matmul(out, invT[:, c, :], vb[:, c, :], start=True, stop=False)
                if c == 1:
                    pe.wait_ge(s_wn, h + 1)
                pe.wait_ge(s_state, 7 * h + c)
                pe.matmul(out, wTn[:, c, :], state[:, :], start=False, stop=True).then_inc(s_vnp, 1)

            def scan_output(h, c):
                out = pt[:, c * P:(c + 1) * P]
                if c:
                    pe.matmul(out, qdT[:, c, :], state[:, :], start=True, stop=False)
                pe.wait_ge(s_vn, 8 * h + c + 1)
                last = pe.matmul(out, attn[:, c, :], vn[c % 2][:, :], start=c == 0, stop=True)
                if c < NT - 1:
                    last = pe.matmul(pt[:, T + HALF:T + HALF + P], kn[:, c, :], vn[c % 2][:, :],
                                     start=True, stop=True)
                last.then_inc(s_kdp, 1)

            def decay_by_columns(h):
                pe.wait_ge(s_gb, h + 1)
                if not peeled(h):
                    pe.wait_ge(s_wn, h)
                for c in range(NT):
                    last = pe.matmul(pm[:, c * P:(c + 1) * P], m1[:, c, :], upper[:, :], start=True, stop=True)
                last.then_inc(s_gcb, 1)

            def turn(out, source):
                for c in range(NT):
                    last = pe.transpose(out[:, c, :], source[:, c, :], ident[:, :])
                return last

            def output_turn(h):
                turn(by_chunk(pt, T), on).then_inc(s_oT, 1)

            def prepare(h):
                project_parts(h, 24, 3)
                pe.wait_ge(s_silu, 3 * h + 2)
                pe.wait_ge(s_dx, 2 * h + 2)
                turn(by_chunk(pm), by_chunk(qkv[1])).then_inc(s_tok, 1)
                pe.wait_ge(s_sq, 2 * h + 2)
                if not peeled(h):
                    pe.wait_ge(s_state, 7 * h)
                for i, squares in enumerate((aT, inv)):
                    for c in range(NT):
                        last = pe.matmul(norms_ps[:, i * NT + c:i * NT + c + 1], squares[:, c, :],
                                         consts["ones"][:, 0:1], start=True, stop=True)
                    if i == 0:
                        project_parts(h, 27, 1)
                last.then_inc(s_ss, 1)
                project_parts(h, 28, 3)
                pe.wait_ge(s_silu, 3 * h + 3)
                pe.wait_ge(s_kc, h + 1)
                turn(by_chunk(pm), by_chunk(qkv[2])).then_inc(s_tok, 1)
                project_parts(h, 31, 1)
                pe.wait_ge(s_std, h + 1)
                if not peeled(h):
                    pe.wait_ge(s_on, h)
                    output_turn(h - 1)
                project_parts(h, 32, 1)
                if not peeled(h):
                    pe.wait_ge(s_og, h)
                for c in range(NT):
                    at = slice(c * P, (c + 1) * P)
                    pe.matmul(pt[:, c * 2 * P:c * 2 * P + P], qkv[1][:, at], qkv[1][:, at], start=True, stop=True)
                    last = pe.matmul(pt[:, c * 2 * P + P:(c + 1) * 2 * P], qkv[1][:, at], qkv[0][:, at],
                                     start=True, stop=True)
                last.then_inc(s_g, 1)
                project_parts(h, 33, 3)
                pe.wait_ge(s_pair, h + 1)
                pe.wait_ge(s_vb, h + 1)
                turn(by_chunk(pm), invT).then_inc(s_pairT, 1)
                project_parts(h, 36, 1)
                pe.wait_ge(s_invc, h + 1)
                pe.wait_ge(s_ap, h + 1)
                for n in range(len(LEVELS)):
                    last_level = n == len(LEVELS) - 1
                    if n % 2:
                        project_parts(h, 37 + n // 2, 1)
                    c_level = cT[n % 2]
                    low, high = slice(0, P // 2), slice(P // 2, P)
                    pe.wait_ge(s_ct, 6 * h + n + 1)
                    for a in range(2):
                        if n:
                            pe.wait_ge(s_t, L * h + 2 * n - 1 + a)
                        for c in range(4 * a, 4 * a + 4):
                            out = by_chunk(pm)[:, c, :]
                            if last_level:
                                last = pe.matmul(out[:, low], c_level[:, c, :], inv[:, c, low],
                                                 start=True, stop=True)
                            else:
                                last = pe.matmul(out, c_level[:, c, :], inv[:, c, :], start=True, stop=True)
                        last.then_inc(s_m1p, 1)
                    for a in range(2):
                        pe.wait_ge(s_m1, L * h + 2 * n + a + 1)
                        for c in range(4):
                            at = a * T + c * P
                            i = 4 * a + c
                            if last_level:
                                last = pe.matmul(pt[:, at + HALF + P // 2:at + HALF + P], m1[:, i, :],
                                                 invT[:, i, high], start=True, stop=True)
                                continue
                            pe.matmul(pt[:, at:at + P], invT[:, i, :], m1[:, i, :], start=True, stop=True)
                            last = pe.matmul(pt[:, at + HALF:at + HALF + P], m1[:, i, :], invT[:, i, :],
                                             start=True, stop=True)
                        last.then_inc(s_x, 1)
                pe.wait_ge(s_t, L * h + L)
                pe.wait_ge(s_kx, 2 * h + 2)
                pe.wait_ge(s_qd, h + 1)
                for c in range(NT):
                    last = pe.matmul(pm[:, c * P:(c + 1) * P], kb[:, c, :], invT[:, c, :], start=True, stop=True)
                last.then_inc(s_w, 1)

            def gate_logits():
                pe.wait_ge(s_gwlo, 1)
                token_logits(pe, logitsT_ps, x_hi, x_lo, gate_hi, gate_lo).then_inc(s_lp, 1)

            def gates_turned():
                pe.wait_ge(s_lc, 1)
                for c in range(NT):
                    last = pe.transpose(logits_ps[:, c, :], logitsT[:, c * P:(c + 1) * P],
                                        ident[0:2 * H, 0:2 * H])
                last.then_inc(s_lt, 1)

            def decays_summed():
                pe.wait_ge(s_gl, 1)
                flat = g_log[:, :, :].rearrange("p h c -> p (h c)")
                pe.matmul(cum_ps, upper[:, :], flat, start=True, stop=True)
                pe.matmul(total_ps, consts["ones"][:, :], flat, start=True, stop=True).then_inc(s_gc, 1)

            def first_project():
                gate_logits()
                project_parts(0, 0, 2)
                gates_turned()
                project_parts(0, 2, 4)
                decays_summed()
                project_parts(0, 6, 2)
                decay_by_columns(0)
                project_parts(0, 8, 16)

            def project_and_scan(h):
                for c in range(NT):
                    scan_value(h - 1, c)
                    project_parts(h, 8 + 2 * c, 1)
                    scan_output(h - 1, c)
                    project_parts(h, 9 + 2 * c, 1)
                    if c == 0:
                        decay_by_columns(h)

            def body(h):
                if peeled(h):
                    first_project()
                else:
                    project_and_scan(h)
                prepare(h)

            def after(h):
                for n in range(NT):
                    scan_value(h - 1, n)
                    scan_output(h - 1, n)
                pe.wait_ge(s_on, h)
                output_turn(h - 1)

            heads(pe, body, after)


GLA_HEADS = 4
GLA_DK = 128
GLA_DV = 256
GLA_RANK = 16
GLA_TILES = 6
GLA_TAU = 16.0


def gla(nc, consts, w_in, w_small, w_up, bias, o_gain, x_hi, x_lo, mixed):
    ident, eps, masks = consts["ident"], consts["eps"], consts["masks"]
    sizes = (64, 32, 16, 8, 4, 2, 1)
    N = len(sizes)
    M = 2 * (N + 1)
    HALVES = 2 * GLA_TILES
    ctx = ExitStack()
    with ctx:
        sb, ps = buffers(nc, ctx)
        sem = semaphores(nc, ctx, "l_")
        H = GLA_HEADS
        raw = [sb(f"l_raw{i}", [P, D]) for i in range(SLOTS)]
        w_hi = [sb(f"l_whi{i}", [P, D], F32R) for i in range(SLOTS)]
        w_lo = [sb(f"l_wlo{i}", [P, D], F32R) for i in range(SLOTS)]
        low_raw = sb("l_lowraw", [P, KT, GLA_RANK])
        low_hi = sb("l_lowhi", [P, KT, GLA_RANK], F32R)
        low_lo = sb("l_lowlo", [P, KT, GLA_RANK], F32R)
        lowT = sb("l_lowT", [GLA_RANK, T])
        up = sb("l_up", [GLA_RANK, GLA_HEADS * P])
        up_head = sb("l_uphead", [GLA_RANK, P])
        b = sb("l_bias", [P, GLA_HEADS])
        keep = sb("l_keep", [P, NT, P])
        qT, kT, bh, attn, tmp, qd, kd = (sb("l_" + x, [P, T]) for x in ("qT", "kT", "bh", "attn", "tmp", "qd", "kd"))
        vT, r, rc, og, ex = ([sb(f"l_{x}{i}", [P, T]) for i in range(2)] for x in ("vT", "r", "rc", "og", "ex"))
        y, absolute = ex
        kt = sb("l_kt", [P, NT, P])
        v = sb("l_v", [P, NT, GLA_DV])
        on = sb("l_on", [P, NT, GLA_DV])
        state = [sb(f"l_state{i}", [P, GLA_DV]) for i in range(2)]
        cd = sb("l_cd", [P, NT])
        sso, stdo, rso = (sb(f"l_{x}", [P, NT]) for x in ("sso", "stdo", "rso"))
        gain = sb("l_gain", [P, 2])
        pa = ps("l_pa", [P, T])
        pm = ps("l_pm", [P, T])
        pt = ps("l_pt", [P, 2 * T])
        lowT_ps = pm[0:GLA_RANK, :]

        def by_chunk(x):
            return x[:, :].rearrange("p (c t) -> p c t", c=NT)

        s_raw = [sem(f"w_raw{i}") for i in range(SLOTS)]
        s_hi, s_lo = sem("w_high"), sem("w_low")
        s_in = sem("constants_loaded")
        s_lraw, s_lhi, s_llo = sem("gate_w_raw"), sem("gate_w_high"), sem("gate_w_low")
        s_lowTp, s_lowT = sem("gate_input_in_psum"), sem("gate_input_copied")
        s_up = sem("gate_w_up_copied")
        s_full, s_y = sem("gate_half_in_psum"), sem("gate_half_biased")
        s_abs, s_ln = sem("gate_absolute_made"), sem("gate_logs_made")
        s_a, s_u = sem("projection_half_done"), sem("projection_half_evicted")
        s_sub, s_exp, s_f = sem("level_exponent_made"), sem("level_exps_made"), sem("level_factors_made")
        s_lp, s_lacc = sem("level_half_product_done"), sem("level_half_product_masked")
        s_end, s_endx = sem("end_exponent_made"), sem("end_exps_made")
        s_qk = sem("queries_keys_decayed")
        s_attn = sem("attention_made")
        s_ktp, s_kt = sem("keys_in_psum"), sem("keys_copied")
        s_vp, s_v = sem("values_in_psum"), sem("values_copied")
        s_rc = sem("gate_activated")
        s_kdp, s_o, s_state = sem("state_product_done"), sem("chunk_output_done"), sem("state_updated")
        s_sqo, s_sso, s_stdo = sem("output_squares_made"), sem("output_squares_summed"), sem("output_deviation")
        s_on, s_oT, s_og, s_ost = sem("output_normed"), sem("output_turned"), sem("output_gated"), sem("output_stored")

        def peeled(h):
            return isinstance(h, int) and h == 0

        block = ctx.enter_context(nc.Block())

        def heads(engine, body, after):
            body(0)
            with engine.Fori(1, H) as h:
                body(h)
            after(H)

        @block.sync
        def _(sp):
            def load(n, k):
                sp.dma_start(raw[k % SLOTS][:, :], w_in[bass.ds(n, 1), :, :].rearrange("a p f -> p (a f)")) \
                    .then_inc(s_raw[k % SLOTS], 16)

            def store(h):
                for j in range(2):
                    sp.wait_ge(s_og, 2 * h + j + 1)
                    sp.dma_start(mixed[bass.ds(2 * h + j, 1), :, :].rearrange("a p t -> p (a t)"), og[j][:, :]) \
                        .then_inc(s_ost, 16)

            sp.dma_start(low_raw[:, :, :], w_small).then_inc(s_lraw, 16)
            load(0, 0)
            load(1, 1)
            sp.dma_start(up[:, :], w_up).then_inc(s_in, 16)
            sp.dma_start(b[:, :], bias).then_inc(s_in, 16)
            sp.dma_start(gain[:, :], o_gain).then_inc(s_in, 16)

            def body(h):
                for k in range(SLOTS, GLA_TILES + SLOTS):
                    sp.wait_ge(s_lo, GLA_TILES * h + k - SLOTS + 1)
                    n = GLA_TILES * h + k
                    load(n if isinstance(h, int) else n % (GLA_TILES * H), k)
                    if k == 5 and not peeled(h):
                        store(h - 1)

            heads(sp, body, lambda h: store(h - 1))
            sp.wait_ge(s_ost, 32 * H)

        @block.gpsimd
        def _(pool):
            def split(h, k):
                pool.wait_ge(s_hi, GLA_TILES * h + k + 1)
                s = k % SLOTS
                pool.tensor_tensor(w_lo[s][:, :], raw[s][:, :], w_hi[s][:, :].bitcast(F32), ALU.subtract) \
                    .then_inc(s_lo, 1)

            def body(h):
                for k in range(SLOTS, GLA_TILES + SLOTS):
                    split(h, k)

            split(0, 0)
            split(0, 1)
            heads(pool, body, lambda h: None)

        @block.scalar
        def _(act):
            def high(h, k):
                act.wait_ge(s_raw[k % SLOTS], 16 * (3 * h + k // 2) + 16)
                if not (peeled(h) and k < SLOTS):
                    act.wait_ge(s_a, HALVES * h + 2 * (k - SLOTS) + 2)
                act.activation(w_hi[k % SLOTS][:, :], raw[k % SLOTS][:, :], ACT.Copy).then_inc(s_hi, 1)

            def evict(h, n):
                act.wait_ge(s_a, HALVES * h + n + 1)
                cols = slice(n % 2 * HALF, (n % 2 + 1) * HALF)
                out = (qT, kT, *vT, *r)[n // 2]
                act.activation(out[:, cols], pa[:, cols], ACT.Copy,
                               scale=float(GLA_DK) ** -0.5 if n < 2 else 1.0).then_inc(s_u, 1)
                if n % 2:
                    high(h, n // 2 + SLOTS)

            def project(h):
                if not peeled(h):
                    act.wait_ge(s_qk, h)
                evict(h, 0)
                evict(h, 1)
                act.wait_ge(s_abs, h + 1)
                act.activation(absolute[:, :], absolute[:, :], ACT.Exp, scale=-1.0)
                act.drain()
                act.activation(absolute[:, :], absolute[:, :], ACT.Ln, bias=consts["ones"][:, 0:1]) \
                    .then_inc(s_ln, 1)
                evict(h, 2)
                evict(h, 3)

            def output_squares(h):
                act.wait_ge(s_o, 8 * h + 8)
                act.activation(on[:, :, :], pt[:, :].rearrange("p (c d) -> p c d", c=NT), ACT.Square) \
                    .then_inc(s_sqo, 1)

            def output_deviation(h):
                act.wait_ge(s_sso, h + 1)
                act.activation(stdo[:, :], sso[:, :], ACT.Sqrt, scale=1.0 / GLA_DV, bias=eps[:, 0:1]) \
                    .then_inc(s_stdo, 1)

            def level_exps(h, n):
                act.wait_ge(s_sub, N * h + n + 1)
                e = ex[n % 2][:, :].rearrange("p (b half t) -> p b half t", half=2, t=sizes[n])
                act.activation(e[:, :, 0, :], e[:, :, 0, :], ACT.Exp, scale=-1.0)
                act.activation(e[:, :, 1, :], e[:, :, 1, :], ACT.Exp)
                act.drain().then_inc(s_exp, 1)

            def end_exps(h):
                act.wait_ge(s_end, h + 1)
                act.activation(qd[:, :], bh[:, :], ACT.Exp)
                act.activation(kd[:, :], kd[:, :], ACT.Exp)
                act.activation(cd[:, :].unsqueeze(2), by_chunk(bh)[:, :, P - 1:P], ACT.Exp)
                act.drain().then_inc(s_endx, 1)

            def prepare(h):
                level_exps(h, 0)
                if not peeled(h):
                    output_deviation(h - 1)
                for m in range(N + 1):
                    if m + 1 < N:
                        level_exps(h, m + 1)
                    if m == 3:
                        end_exps(h)
                    if m == N:
                        act.wait_ge(s_vp, h + 1)
                        act.activation(v[:, :, :], pt[:, :].rearrange("p (c d) -> p c d", c=NT), ACT.Copy) \
                            .then_inc(s_v, 1)
                    evict(h, 4 + m)
                act.wait_ge(s_ktp, h + 1)
                act.activation(kt[:, :, :], by_chunk(pm), ACT.Copy).then_inc(s_kt, 1)
                act.drain()
                for j in range(2):
                    act.activation(rc[j][:, :], r[j][:, :], ACT.Silu)
                act.drain().then_inc(s_rc, 1)

            act.wait_ge(s_lraw, 16)
            act.activation(low_hi[:, :, :], low_raw[:, :, :], ACT.Copy).then_inc(s_lhi, 1)
            high(0, 0)
            high(0, 1)

            def body(h):
                project(h)
                if not peeled(h):
                    output_squares(h - 1)
                prepare(h)

            heads(act, body, lambda h: (output_squares(h - 1), output_deviation(h - 1)))

        @block.vector
        def _(dve):
            def update_state(h, c):
                dve.drain()
                dve.wait_ge(s_kdp, 7 * h + c + 1)
                out, psum = state[(c + 1) % 2], pm[:, c % 2 * HALF:c % 2 * HALF + GLA_DV]
                if c == 0:
                    dve.tensor_copy(out[:, :], psum).then_inc(s_state, 1)
                    return
                dve.wait_ge(s_o, 8 * h + c)
                dve.scalar_tensor_tensor(out=out[:, :], in0=state[c % 2][:, :], scalar=cd[:, c:c + 1], in1=psum,
                                         op0=ALU.mult, op1=ALU.add).then_inc(s_state, 1)

            def gate_biased(h, half):
                cols = slice(half * HALF, (half + 1) * HALF)
                dve.drain()
                dve.wait_ge(s_full, 2 * h + half + 1)
                dve.tensor_scalar(y[:, cols], pa[:, cols], b[:, bass.ds(h, 1)], None, ALU.add).then_inc(s_y, 1)

            def gate_absolute(h):
                dve.drain()
                dve.scalar_tensor_tensor(out=absolute[:, :], in0=y[:, :], scalar=-1.0, in1=y[:, :], op0=ALU.mult,
                                         op1=ALU.max).then_inc(s_abs, 1)

            def gate_summed(h):
                dve.wait_ge(s_ln, h + 1)
                dve.scalar_tensor_tensor(out=y[:, :], in0=y[:, :], scalar=0.0, in1=absolute[:, :], op0=ALU.min,
                                         op1=ALU.subtract)
                dve.drain()
                dve.tensor_tensor_scan(out=tmp[:, :], data0=keep[:, :, :].rearrange("p c t -> p (c t)"),
                                       data1=y[:, :], initial=0.0, op0=ALU.mult, op1=ALU.add)
                dve.drain()
                dve.tensor_scalar(bh[:, :], tmp[:, :], 1.0 / GLA_TAU, None, ALU.mult)
                dve.drain()

            def level_exponent(h, n):
                s = sizes[n]
                blocks = bh[:, :].rearrange("p (b t) -> p b t", t=2 * s)
                middle = blocks[:, :, s - 1:s].to_broadcast([P, T // (2 * s), 2 * s])
                if n >= 2:
                    dve.wait_ge(s_lp, M * h + 2 * n)
                dve.tensor_tensor(ex[n % 2][:, :].rearrange("p (b t) -> p b t", t=2 * s), blocks, middle,
                                  ALU.subtract).then_inc(s_sub, 1)

            def level_factors(h, n):
                s = sizes[n]
                e, q, k = (x[:, :].rearrange("p (b half t) -> p b half t", half=2, t=s) for x in (ex[n % 2], qT, kT))
                dve.wait_ge(s_exp, N * h + n + 1)
                dve.tensor_tensor(e[:, :, 0, :], e[:, :, 0, :], k[:, :, 0, :], ALU.mult)
                dve.tensor_tensor(e[:, :, 1, :], e[:, :, 1, :], q[:, :, 1, :], ALU.mult)
                dve.drain().then_inc(s_f, 1)

            def level_add(h, m):
                out, mask = (attn, ident[:, :]) if m == 0 else (tmp, masks[:, N - m, :])
                dve.drain()
                for a in range(2):
                    dve.wait_ge(s_lp, M * h + 2 * m + a + 1)
                    dve.tensor_tensor(by_chunk(out)[:, 4 * a:4 * a + 4, :], by_chunk(pm)[:, 4 * a:4 * a + 4, :],
                                      each(mask, 4), ALU.mult).then_inc(s_lacc, 1)
                if m:
                    dve.drain()
                    ins = dve.tensor_tensor(attn[:, :], attn[:, :], tmp[:, :], ALU.add)
                    if m == N:
                        ins.then_inc(s_attn, 1)

            def output_sums(h):
                dve.wait_ge(s_sqo, h + 1)
                dve.tensor_reduce(out=sso[:, :], in_=on[:, :, :], axis=AX_X, op=ALU.add).then_inc(s_sso, 1)

            def output_norm(h):
                dve.wait_ge(s_stdo, h + 1)
                dve.reciprocal(rso[:, :], stdo[:, :])
                dve.drain()
                dve.tensor_tensor(on[:, :, :], pt[:, :].rearrange("p (c d) -> p c d", c=NT),
                                  wide(rso[:, :], GLA_DV), ALU.mult).then_inc(s_on, 1)

            def output_gate(h):
                dve.wait_ge(s_rc, h + 1)
                if not (isinstance(h, int) and h == 0):
                    dve.wait_ge(s_ost, 32 * h)
                dve.wait_ge(s_oT, h + 1)
                for j in range(2):
                    dve.scalar_tensor_tensor(out=og[j][:, :], in0=pt[:, j * T:(j + 1) * T], scalar=gain[:, j:j + 1],
                                             in1=rc[j][:, :], op0=ALU.mult, op1=ALU.mult).then_inc(s_og, 1)

            def decayed(h):
                dve.wait_ge(s_endx, h + 1)
                dve.tensor_tensor(qd[:, :], qd[:, :], qT[:, :], ALU.mult)
                dve.tensor_tensor(kd[:, :], kd[:, :], kT[:, :], ALU.mult)
                dve.drain().then_inc(s_qk, 1)

            def project(h):
                scans = not peeled(h)
                dve.tensor_copy(up_head[:, :], up[:, bass.ds(h * P, P)]).then_inc(s_up, 1)
                for c in range(4):
                    if scans:
                        update_state(h - 1, c)
                gate_biased(h, 0)
                if scans:
                    update_state(h - 1, 4)
                gate_biased(h, 1)
                gate_absolute(h)
                if scans:
                    update_state(h - 1, 5)
                gate_summed(h)
                if scans:
                    update_state(h - 1, 6)
                level_exponent(h, 0)
                level_exponent(h, 1)

            def prepare(h):
                b = by_chunk(bh)
                dve.tensor_tensor(by_chunk(kd), b[:, :, P - 1:P].to_broadcast([P, NT, P]), b, ALU.subtract) \
                    .then_inc(s_end, 1)
                if not peeled(h):
                    output_sums(h - 1)
                level_add(h, 0)
                for n in range(N):
                    if n:
                        if n < N - 1:
                            dve.drain()
                            level_exponent(h, n + 1)
                    level_factors(h, n)
                    if n == 0 and not peeled(h):
                        output_norm(h - 1)
                    if n:
                        level_add(h, n)
                    if n == 3 and not peeled(h):
                        output_gate(h - 1)
                    if n == 5:
                        decayed(h)
                level_add(h, N)

            dve.wait_ge(s_lhi, 1)
            dve.tensor_tensor(low_lo[:, :, :], low_raw[:, :, :], low_hi[:, :, :].bitcast(F32), ALU.subtract) \
                .then_inc(s_llo, 1)
            dve.memset(keep[:, :, :], 1.0)
            dve.drain()
            dve.memset(keep[:, :, 0:1], 0.0)
            dve.wait_ge(s_lowTp, 1)
            dve.tensor_copy(lowT[:, :], lowT_ps).then_inc(s_lowT, 1)
            dve.wait_ge(s_in, 48)

            def body(h):
                project(h)
                prepare(h)

            def after(h):
                for c in range(NT - 1):
                    update_state(h - 1, c)
                output_sums(h - 1)
                output_norm(h - 1)
                output_gate(h - 1)

            heads(dve, body, after)

        @block.tensor
        def _(pe):
            def project_half(h, n):
                k = n // 2
                s = k % SLOTS
                cols = slice(n % 2 * HALF, (n % 2 + 1) * HALF)
                pe.wait_ge(s_lo, GLA_TILES * h + k + 1)
                if n in (2, 3):
                    pe.wait_ge(s_y, 2 * h + n - 1)
                elif not (peeled(h) and n < 2):
                    pe.wait_ge(s_u, HALVES * h + n - 1)
                for kt_ in range(KT):
                    f = slice(kt_ * P, (kt_ + 1) * P)
                    last = product3(pe, pa[:, cols], w_hi[s][:, f], w_lo[s][:, f], x_hi[:, kt_, cols],
                                    x_lo[:, kt_, cols], kt_ == 0, kt_ == KT - 1)
                last.then_inc(s_a, 1)

            def gate_half(h, half):
                cols = slice(half * HALF, (half + 1) * HALF)
                pe.wait_ge(s_u, HALVES * h + half + 1)
                pe.wait_ge(s_up, h + 1)
                pe.matmul(pa[:, cols], up_head[:, :], lowT[:, cols], start=True, stop=True).then_inc(s_full, 1)

            def scan_chunk(h, c):
                if c == 0:
                    pe.wait_ge(s_kt, h + 1)
                    pe.wait_ge(s_v, h + 1)
                    pe.wait_ge(s_attn, h + 1)
                if c < NT - 1:
                    if c >= 2:
                        pe.wait_ge(s_state, 7 * h + c - 1)
                    pe.matmul(pm[:, c % 2 * HALF:c % 2 * HALF + GLA_DV], kt[:, c, :], v[:, c, :],
                              start=True, stop=True).then_inc(s_kdp, 1)
                out = pt[:, c * GLA_DV:(c + 1) * GLA_DV]
                if c:
                    pe.wait_ge(s_state, 7 * h + c)
                    pe.matmul(out, by_chunk(qd)[:, c, :], state[c % 2][:, :], start=True, stop=False)
                pe.matmul(out, by_chunk(attn)[:, c, :], v[:, c, :], start=c == 0, stop=True).then_inc(s_o, 1)

            def turn(out, source):
                for c in range(NT):
                    last = pe.transpose(out[:, c, :], source[:, c, :], ident[:, :])
                return last

            def output_turn(h):
                pe.wait_ge(s_on, h + 1)
                for j in range(2):
                    last = turn(pt[:, j * T:(j + 1) * T].rearrange("p (c t) -> p c t", c=NT),
                                on[:, :, j * P:(j + 1) * P])
                last.then_inc(s_oT, 1)

            def level_product(h, m):
                if m == 0:
                    pe.wait_ge(s_u, HALVES * h + 4)
                    if not peeled(h):
                        pe.wait_ge(s_state, 7 * h)
                else:
                    pe.wait_ge(s_f, N * h + m)
                e = ex[(m - 1) % 2]
                a, b = (kT, qT) if m == 0 else (e, e)
                for half in range(2):
                    if m:
                        pe.wait_ge(s_lacc, M * h + 2 * m + half - 1)
                    for c in range(4 * half, 4 * half + 4):
                        last = pe.matmul(by_chunk(pm)[:, c, :], by_chunk(a)[:, c, :], by_chunk(b)[:, c, :],
                                         start=True, stop=True)
                    last.then_inc(s_lp, 1)

            def project(h):
                scans = not peeled(h)
                project_half(h, 0)
                if scans:
                    scan_chunk(h - 1, 0)
                    scan_chunk(h - 1, 1)
                project_half(h, 1)
                if scans:
                    scan_chunk(h - 1, 2)
                    scan_chunk(h - 1, 3)
                else:
                    pe.wait_ge(s_lowT, 1)
                gate_half(h, 0)
                if scans:
                    scan_chunk(h - 1, 4)
                gate_half(h, 1)
                if scans:
                    scan_chunk(h - 1, 5)
                project_half(h, 2)
                if scans:
                    scan_chunk(h - 1, 6)
                    scan_chunk(h - 1, 7)
                project_half(h, 3)

            def prepare(h):
                for m in range(N + 1):
                    level_product(h, m)
                    if m == 2 and not peeled(h):
                        output_turn(h - 1)
                    if m == N - 1:
                        if not peeled(h):
                            pe.wait_ge(s_og, 2 * h)
                        pe.wait_ge(s_u, HALVES * h + 8)
                        for j in range(2):
                            last = turn(pt[:, :].rearrange("p (c d) -> p c d", c=NT)[:, :, j * P:(j + 1) * P],
                                        by_chunk(vT[j]))
                        last.then_inc(s_vp, 1)
                    project_half(h, 4 + m)
                pe.wait_ge(s_qk, h + 1)
                pe.wait_ge(s_lacc, M * h + M)
                turn(by_chunk(pm), by_chunk(kd)).then_inc(s_ktp, 1)

            def body(h):
                project(h)
                prepare(h)

            def after(h):
                for n in range(NT):
                    scan_chunk(h - 1, n)
                output_turn(h - 1)

            pe.wait_ge(s_llo, 1)
            token_logits(pe, lowT_ps, x_hi, x_lo, low_hi, low_lo).then_inc(s_lowTp, 1)
            heads(pe, body, after)




def build_program(nc, x, gdn_w_in, gdn_w_gates, gdn_conv_w, gdn_a_log, gdn_dt_bias, gdn_o_gain, gdn_w_out,
                  gla_w_in, gla_w_low, gla_w_up, gla_bias, gla_o_gain, gla_w_out, mix_pre, mix_post, ffn_pre,
                  ffn_post, ffn_w_up, ffn_conv_w, ffn_w_down, out):
    x_mid = [nc.dram_tensor(f"x_mid{i}", (NT, P, D), F32, kind="Internal").ap() for i in range(3)]
    mixed = nc.dram_tensor("mixed", (KT, P, T), F32, kind="Internal").ap()
    with ExitStack() as ctx:
        consts = constants(nc, ctx)
        sb, _ = buffers(nc, ctx)
        x_hi = sb("x_hi", [P, KT, T], F32R)
        x_lo = sb("x_lo", [P, KT, T], F32R)

        def feed_forward(layer, x_in, x_out, pre_gain):
            with nc.sbuf_tensor(f"acc{layer}", [P, NT, D], F32) as acc:
                with ExitStack() as stack:
                    lead = ffn(nc, stack, layer, ffn_w_up, ffn_conv_w, ffn_w_down, x_hi, x_lo, acc)
                    token_pass(nc, f"after_ffn{layer}", consts, x_in, x_out, ffn_post[layer:layer + 1, :],
                               pre_gain, x_hi, x_lo, acc=acc, lead=lead)

        token_pass(nc, "first", consts, x, None, None, mix_pre[0:1, :], x_hi, x_lo)
        gdn(nc, consts, gdn_w_in, gdn_w_gates, gdn_conv_w, gdn_a_log, gdn_dt_bias, gdn_o_gain, x_hi, x_lo, mixed)
        token_pass(nc, "after_gdn", consts, x, x_mid[0], mix_post[0:1, :], ffn_pre[0:1, :], x_hi, x_lo,
                   mixed=mixed, w_out=gdn_w_out)
        feed_forward(0, x_mid[0], x_mid[1], mix_pre[1:2, :])
        gla(nc, consts, gla_w_in, gla_w_low, gla_w_up, gla_bias, gla_o_gain, x_hi, x_lo, mixed)
        token_pass(nc, "after_gla", consts, x_mid[1], x_mid[2], mix_post[1:2, :], ffn_pre[1:2, :], x_hi, x_lo,
                   mixed=mixed, w_out=gla_w_out)
        feed_forward(1, x_mid[2], out, None)


def kernel(**inputs):
    import numpy as np
    import concourse.bacc as bacc
    from concourse.bass_utils import run_bass_kernel_spmd

    a = {name: np.asarray(value) for name, value in inputs.items()}

    def tiles(w):
        return w.reshape(KT, P, -1, P).transpose(2, 1, 0, 3).reshape(-1, P, D)

    def by_partition(v):
        return np.swapaxes(v.reshape(*v.shape[:-1], -1, P), -1, -2)

    gdn_w = a["gdn_w_in"][0]
    gdn_cols = 4 * GDN_HEADS * P
    gdn_tiles = tiles(gdn_w[:, :gdn_cols]).reshape(4, GDN_HEADS, P, D).transpose(1, 0, 2, 3).reshape(-1, P, D)
    gla_w = a["gla_w_in"][0]
    gla_cols = GLA_TILES * GLA_HEADS * P
    t = tiles(gla_w[:, :gla_cols])
    n = GLA_HEADS
    gla_tiles = np.stack([t[i] for h in range(n) for i in
                          (h, n + h, 2 * n + 2 * h, 2 * n + 2 * h + 1, 4 * n + 2 * h, 4 * n + 2 * h + 1)])
    taps = a["gdn_conv_w"][0].reshape(GDN_TAPS, 3, GDN_HEADS, P).transpose(3, 2, 1, 0)
    depth = a["ffn_w_up"].shape[0]
    arrays = {
        "x": a["x"].reshape(NT, P, D),
        "gdn_w_in": gdn_tiles,
        "gdn_w_gates": gdn_w[:, gdn_cols:].reshape(KT, P, -1).transpose(1, 0, 2),
        "gdn_conv_w": taps.reshape(P, 3 * GDN_HEADS, GDN_TAPS),
        "gdn_a_log": a["gdn_a_log"],
        "gdn_dt_bias": a["gdn_dt_bias"],
        "gdn_o_gain": by_partition(a["gdn_o_norm"][0]),
        "gdn_w_out": a["gdn_w_out"][0].reshape(KT, P, D),
        "gla_w_in": gla_tiles,
        "gla_w_low": gla_w[:, gla_cols:].reshape(KT, P, -1).transpose(1, 0, 2),
        "gla_w_up": a["gla_w_gate_up"][0],
        "gla_bias": by_partition(a["gla_gate_bias"][0]),
        "gla_o_gain": by_partition(a["gla_o_norm"][0]),
        "gla_w_out": a["gla_w_out"][0].reshape(KT, P, D),
        "mix_pre": a["mix_pre_norm"],
        "mix_post": a["mix_post_norm"],
        "ffn_pre": a["ffn_pre_norm"],
        "ffn_post": a["ffn_post_norm"],
        "ffn_w_up": np.stack([tiles(w) for w in a["ffn_w_up"]]),
        "ffn_conv_w": a["ffn_conv_w"].reshape(depth, FFN_TAPS, UP_TILES, P).transpose(0, 3, 2, 1),
        "ffn_w_down": a["ffn_w_down"].reshape(depth, FT, P, D),
    }
    arrays = {f"in_{name}": np.ascontiguousarray(value) for name, value in arrays.items()}
    nc = bacc.Bacc("TRN2", target_bir_lowering=False, num_devices=1)
    args = [nc.dram_tensor(name, value.shape, mybir.dt.from_np(value.dtype), kind="ExternalInput").ap()
            for name, value in arrays.items()]
    out = nc.dram_tensor("out", (NT, P, D), F32, kind="ExternalOutput").ap()
    build_program(nc, *args, out)
    result = run_bass_kernel_spmd(nc, [arrays], core_ids=[0])
    return result.results[0]["out"].reshape(1, T, D)
```
